# Optimizing a Trainium2 kernel written in Bass

```python
import math
import jax
import jax.numpy as jnp
from jax import lax
import numpy as np

D_MODEL = 1024
BATCH = 1
SEQ = 256
DEPTH = 2

N_HEADS = 16
N_KV_HEADS = 4
HEAD_DIM = 64
GROUP = N_HEADS // N_KV_HEADS
WINDOW = 128
BLOCK = 128
ATTN_W = N_HEADS * HEAD_DIM
KV_W = N_KV_HEADS * HEAD_DIM
NUM_BUCKETS = 32
MAX_DISTANCE = 128
MAX_EXACT = NUM_BUCKETS // 2
D_RNN = D_MODEL
N_LRU_BLOCKS = 16
LRU_BLOCK = D_RNN // N_LRU_BLOCKS
CONV_WIDTH = 4
LRU_C = 8.0
D_FF = D_MODEL * 7 // 2
N_EXPERTS = 8
TOP_K = 2
N_DENSE = (DEPTH + 1) // 2
N_MOE = DEPTH // 2
PLE_DIM = 256
IN_SPLITS = (ATTN_W, KV_W, KV_W, D_RNN, D_RNN, D_MODEL, D_MODEL)
N_IN = sum(IN_SPLITS)
EPS = 1e-6
NEG_INF = -1e30

kernel_name = "hybrid_swa_rglru_moe_trunk"

def rmsnorm(x, g):
    xf = x.astype(jnp.float32)
    y = xf * lax.rsqrt(jnp.mean(xf * xf, axis=-1, keepdims=True) + EPS)
    return (y * g.astype(jnp.float32)).astype(x.dtype)

def t5_bucket(dist):
    d = jnp.maximum(dist, 0)
    large = MAX_EXACT + (jnp.log(jnp.maximum(d, 1).astype(jnp.float32) / MAX_EXACT)
                         / math.log(MAX_DISTANCE / MAX_EXACT)
                         * (NUM_BUCKETS - MAX_EXACT)).astype(jnp.int32)
    large = jnp.minimum(large, NUM_BUCKETS - 1)
    return jnp.where(d < MAX_EXACT, d, large)

def band_geometry(n_blocks):
    qi = jnp.arange(BLOCK, dtype=jnp.int32)[:, None]
    ks = jnp.arange(2 * BLOCK, dtype=jnp.int32)[None, :]
    dist = BLOCK + qi - ks
    in_window = (dist >= 0) & (dist < WINDOW)
    key_abs = jnp.arange(n_blocks, dtype=jnp.int32)[:, None, None] * BLOCK - BLOCK + ks[None]
    mask = in_window[None] & (key_abs >= 0)
    return t5_bucket(dist), mask

def head_rms(x, g):
    return rmsnorm(x, g)

def sliding_window_attention(q, k, v, bias, mask, sink):
    B, S = q.shape[0], q.shape[1]
    nb = S // BLOCK
    qb = q.reshape(B, nb, BLOCK, N_KV_HEADS, GROUP, HEAD_DIM)

    def band(t):
        tb = t.reshape(B, nb, BLOCK, N_KV_HEADS, HEAD_DIM)
        prev = jnp.pad(tb[:, :-1], ((0, 0), (1, 0), (0, 0), (0, 0), (0, 0)))
        return jnp.concatenate([prev, tb], axis=2)

    kb, vb = band(k), band(v)
    s = jnp.einsum('bnqkgd,bnskd->bnkgqs', qb, kb).astype(jnp.float32) * (HEAD_DIM ** -0.5)
    s = jnp.where(mask[None, :, None, None], s + bias[None, None].astype(jnp.float32), NEG_INF)
    sink_l = sink.astype(jnp.float32).reshape(1, 1, N_KV_HEADS, GROUP, 1, 1)
    m = jnp.maximum(jnp.max(s, axis=-1, keepdims=True), sink_l)
    e = jnp.exp(s - m)
    probs = e / (jnp.sum(e, axis=-1, keepdims=True) + jnp.exp(sink_l - m))
    o = jnp.einsum('bnkgqs,bnskd->bnqkgd', probs.astype(v.dtype), vb)
    return o.reshape(B, S, ATTN_W)

def block_diag(x, w, b):
    B, S, C = x.shape
    xb = x.reshape(B, S, N_LRU_BLOCKS, LRU_BLOCK)
    return (jnp.einsum('bsnc,ncd->bsnd', xb, w) + b).reshape(B, S, C)

def rg_lru_branch(xb, gb, conv_w, conv_b, w_rg, b_rg, w_ig, b_ig, lam):
    C = xb.shape[-1]
    xc = lax.conv_general_dilated(xb, conv_w[:, None, :], window_strides=(1,),
                                  padding=[(CONV_WIDTH - 1, 0)],
                                  dimension_numbers=('NWC', 'WIO', 'NWC'),
                                  feature_group_count=C) + conv_b
    r = jax.nn.sigmoid(block_diag(xc, w_rg, b_rg))
    i = jax.nn.sigmoid(block_diag(xc, w_ig, b_ig))
    log_a = -LRU_C * r.astype(jnp.float32) * jax.nn.softplus(-lam.astype(jnp.float32))
    a = jnp.exp(log_a)
    u = jnp.sqrt(-jnp.expm1(2.0 * log_a)) * (i * xc).astype(jnp.float32)

    def combine(left, right):
        a1, b1 = left
        a2, b2 = right
        return a1 * a2, a2 * b1 + b2

    _, h = lax.associative_scan(combine, (a, u), axis=1)
    return h.astype(xb.dtype) * jax.nn.gelu(gb)

def swiglu(x, w1, w3, w2):
    return (jax.nn.silu(x @ w1) * (x @ w3)) @ w2

def moe_ffn(xn, router_w, router_b, w1, w3, w2):
    logits = (xn @ router_w).astype(jnp.float32) + router_b.astype(jnp.float32)
    top_v, top_i = lax.top_k(logits, TOP_K)
    w = jax.nn.softmax(top_v, axis=-1)
    gate = jnp.sum(jax.nn.one_hot(top_i, N_EXPERTS, dtype=jnp.float32) * w[..., None], axis=-2)
    gate = gate.astype(xn.dtype)
    out = jnp.zeros_like(xn)
    for e in range(N_EXPERTS):
        out = out + gate[..., e:e + 1] * swiglu(xn, w1[e], w3[e], w2[e])
    return out

def setup_inputs(seed: int = 0) -> dict:
    key = jax.random.key(seed)
    keys = iter(jax.random.split(key, 40))
    f32 = jnp.float32

    def nrm(shape, fan_in):
        return jax.random.normal(next(keys), shape, f32) * (fan_in ** -0.5)

    def gain(shape):
        return 1.0 + 0.01 * jax.random.normal(next(keys), shape, f32)

    def small(shape, scale=0.01):
        return scale * jax.random.normal(next(keys), shape, f32)

    x = jax.random.normal(next(keys), (BATCH, SEQ, D_MODEL), f32)
    p = jax.random.normal(next(keys), (DEPTH, BATCH, SEQ, PLE_DIM), f32)
    mix_norm = gain((DEPTH, D_MODEL))
    w_in = nrm((DEPTH, D_MODEL, N_IN), D_MODEL)
    q_norm = gain((DEPTH, HEAD_DIM))
    k_norm = gain((DEPTH, HEAD_DIM))
    sinks = small((DEPTH, N_HEADS), 0.5)
    rel_bias = small((NUM_BUCKETS, N_HEADS), 0.5)
    conv_w = nrm((DEPTH, CONV_WIDTH, D_RNN), CONV_WIDTH)
    conv_b = small((DEPTH, D_RNN))
    w_rg = nrm((DEPTH, N_LRU_BLOCKS, LRU_BLOCK, LRU_BLOCK), LRU_BLOCK)
    b_rg = small((DEPTH, N_LRU_BLOCKS, LRU_BLOCK))
    w_ig = nrm((DEPTH, N_LRU_BLOCKS, LRU_BLOCK, LRU_BLOCK), LRU_BLOCK)
    b_ig = small((DEPTH, N_LRU_BLOCKS, LRU_BLOCK))
    a_c = jax.random.uniform(next(keys), (DEPTH, D_RNN), f32, 0.9, 0.999)
    sig_l = a_c ** (1.0 / LRU_C)
    lru_lambda = jnp.log(sig_l) - jnp.log1p(-sig_l)
    w_proj_attn = nrm((DEPTH, ATTN_W, D_MODEL), ATTN_W)
    w_proj_lru = nrm((DEPTH, D_RNN, D_MODEL), D_RNN)
    w_out = nrm((DEPTH, D_MODEL, D_MODEL), D_MODEL)
    ffn_norm = gain((DEPTH, D_MODEL))
    dense_w1 = nrm((N_DENSE, D_MODEL, D_FF), D_MODEL)
    dense_w3 = nrm((N_DENSE, D_MODEL, D_FF), D_MODEL)
    dense_w2 = nrm((N_DENSE, D_FF, D_MODEL), D_FF)
    router_w = nrm((N_MOE, D_MODEL, N_EXPERTS), D_MODEL)
    router_b = small((N_MOE, N_EXPERTS))
    moe_w1 = nrm((N_MOE, N_EXPERTS, D_MODEL, D_FF), D_MODEL)
    moe_w3 = nrm((N_MOE, N_EXPERTS, D_MODEL, D_FF), D_MODEL)
    moe_w2 = nrm((N_MOE, N_EXPERTS, D_FF, D_MODEL), D_FF)
    ple_norm = gain((DEPTH, D_MODEL))
    ple_gate_w = nrm((DEPTH, D_MODEL, D_MODEL), D_MODEL)
    ple_proj_w = nrm((DEPTH, PLE_DIM, D_MODEL), PLE_DIM)
    return {"x": x, "p": p, "mix_norm": mix_norm, "w_in": w_in, "q_norm": q_norm,
            "k_norm": k_norm, "sinks": sinks, "rel_bias": rel_bias, "conv_w": conv_w,
            "conv_b": conv_b, "w_rg": w_rg, "b_rg": b_rg, "w_ig": w_ig, "b_ig": b_ig,
            "lru_lambda": lru_lambda, "w_proj_attn": w_proj_attn, "w_proj_lru": w_proj_lru,
            "w_out": w_out, "ffn_norm": ffn_norm, "dense_w1": dense_w1, "dense_w3": dense_w3,
            "dense_w2": dense_w2, "router_w": router_w, "router_b": router_b,
            "moe_w1": moe_w1, "moe_w3": moe_w3, "moe_w2": moe_w2, "ple_norm": ple_norm,
            "ple_gate_w": ple_gate_w, "ple_proj_w": ple_proj_w}

def reference(x, p, mix_norm, w_in, q_norm, k_norm, sinks, rel_bias, conv_w, conv_b,
              w_rg, b_rg, w_ig, b_ig, lru_lambda, w_proj_attn, w_proj_lru, w_out,
              ffn_norm, dense_w1, dense_w3, dense_w2, router_w, router_b,
              moe_w1, moe_w3, moe_w2, ple_norm, ple_gate_w, ple_proj_w):
    B, S, _ = x.shape
    nb = S // BLOCK
    bucket, mask = band_geometry(nb)
    bias = jnp.transpose(rel_bias[bucket], (2, 0, 1)).reshape(N_KV_HEADS, GROUP, BLOCK, 2 * BLOCK)
    split_points = list(np.cumsum(IN_SPLITS)[:-1])

    h = x
    for i in range(DEPTH):
        xn = rmsnorm(h, mix_norm[i])
        u = xn @ w_in[i]
        q, k, v, lx, lg, ga, gb = jnp.split(u, split_points, axis=-1)
        q = head_rms(q.reshape(B, S, N_HEADS, HEAD_DIM), q_norm[i])
        k = head_rms(k.reshape(B, S, N_KV_HEADS, HEAD_DIM), k_norm[i])
        v = v.reshape(B, S, N_KV_HEADS, HEAD_DIM)
        y_a = sliding_window_attention(q, k, v, bias, mask, sinks[i])
        y_b = rg_lru_branch(lx, lg, conv_w[i], conv_b[i], w_rg[i], b_rg[i],
                            w_ig[i], b_ig[i], lru_lambda[i])
        merged = (jax.nn.sigmoid(ga) * (y_a @ w_proj_attn[i])
                  + jax.nn.sigmoid(gb) * (y_b @ w_proj_lru[i]))
        h = h + merged @ w_out[i]
        xn2 = rmsnorm(h, ffn_norm[i])
        j = i // 2
        if i % 2 == 0:
            h = h + swiglu(xn2, dense_w1[j], dense_w3[j], dense_w2[j])
        else:
            h = h + moe_ffn(xn2, router_w[j], router_b[j], moe_w1[j], moe_w3[j], moe_w2[j])
        xn3 = rmsnorm(h, ple_norm[i])
        h = h + jax.nn.sigmoid(xn3 @ ple_gate_w[i]) * (p[i] @ ple_proj_w[i])
    return h


_drawn_inputs = setup_inputs


def setup_inputs(seed=0):
    import zlib

    import numpy as np

    out = dict(_drawn_inputs(seed))
    spreads = {}
    factors = {'mix_norm': 5.913,
     'q_norm': 4.828,
     'k_norm': 8.0,
     'sinks': 11.14,
     'b_rg': 8.0,
     'b_ig': 8.0,
     'ffn_norm': 9.896,
     'ple_norm': 200.0,
     'conv_b': 2.72,
     'router_b': 27.068,
     'ple_gate_w': 3.664}
    for name, (base, spread) in spreads.items():
        noise = np.random.default_rng([zlib.crc32(name.encode()), seed]).standard_normal(out[name].shape)
        drawn = base * np.exp(spread * noise) if base else spread * noise
        out[name] = jnp.asarray(drawn.astype(out[name].dtype))
    for name, factor in factors.items():
        out[name] = (out[name] * factor).astype(out[name].dtype)
    return out
```

```python
import math
from contextlib import ExitStack

import numpy as np

import concourse.bass as bass
from concourse import mybir

F32 = mybir.dt.float32
I32 = mybir.dt.int32
ALU = mybir.AluOpType
ACT = mybir.ActivationFunctionType
AX_X = mybir.AxisListType.X

P = 128
D = 1024
T = 256
DEPTH = 2
KT = D // P
TT = T // P
HEADS = 16
KV_HEADS = 4
HD = 64
PAIRS = HEADS // 2
BAND = 256
WINDOW = 128
BUCKETS = 32
MAX_EXACT = BUCKETS // 2
MAX_DISTANCE = 128
CONV = 4
LRU_C = 8.0
LRU_BLOCKS = 16
D_FF = D * 7 // 2
EXPERTS = 8
PLE = 256
EPS = 1e-6
MASKED = -1e30
CW = 512
CHUNK = KT * CW
FT = CW // P
FC = D_FF // CW
RING = 7
MIX_RING = 6
MIX_CHUNKS = 17
FFN_CHUNKS = 3 * FC
PLE_CHUNKS = 2
U_LEN = 384

W_IN_ORDER = [0, 1, 2, 3, 4, 9, 10, 7, 8]
W_IN_LG = [5, 6]


def bucket_of(dist):
    if dist < MAX_EXACT:
        return dist
    f = np.float32(np.log(np.float32(dist) / np.float32(MAX_EXACT)))
    f = np.float32(f / np.float32(math.log(MAX_DISTANCE / MAX_EXACT))) * np.float32(BUCKETS - MAX_EXACT)
    return min(MAX_EXACT + int(f), BUCKETS - 1)


def ffn_order():
    order = []
    for c in range(FC):
        order += [("w1", c), ("w3", c)]
        if c:
            order.append(("w2", c - 1))
    return order + [("w2", FC - 1)]


def mixer_groups():
    groups = [("qkv", c, tt) for c in range(3) for tt in range(TT)]
    for name in ("lx", "gb", "ga", "pa", "lg", "pb", "out"):
        groups += [(name, j) for j in range(KT)]
    return groups


class Steps:

    def __init__(self, eng, sem):
        self.eng, self.sem, self.n = eng, sem, 0

    def __call__(self, ins):
        self.n += 1
        ins.then_inc(self.sem, 1)

    def settle(self):
        self.eng.wait_ge(self.sem, self.n)


def trunk(nc, xT, pT, cols, rows, relT, wrg_d, wig_d, router_d, mix_w, dense_w, moe_w, ple_w, ple_p, bias_line, outT):
    groups = []
    for l in range(DEPTH):
        groups += [(l, *g) for g in mixer_groups()]
        if l % 2 == 0:
            groups += [(l, "ffn", c, ft) for c in range(FC) for ft in range(FT)]
        groups += [(l, "ple", j) for j in range(KT)]
    place = {g: (i % 2, i // 2) for i, g in enumerate(groups)}

    uses = [0] * RING
    at = {}

    def put(key, slot):
        at[key] = (slot, uses[slot])
        uses[slot] += 1

    moe_base = None
    for l in range(DEPTH):
        for i in range(MIX_CHUNKS):
            put((l, "mix", i), i % MIX_RING)
        if l % 2 == 0:
            for i, (w, c) in enumerate(ffn_order()):
                put((l, w, c), i % RING)
        else:
            moe_base = list(uses)
            uses = [u + EXPERTS * FFN_CHUNKS // RING for u in uses]
        for i in range(PLE_CHUNKS + 1):
            put((l, "ple", i), i % MIX_RING)
    FFN_AT = {wc: i for i, wc in enumerate(ffn_order())}

    with ExitStack() as ctx:
        def sb(name, shape, dt=F32):
            return ctx.enter_context(nc.sbuf_tensor(name, shape, dt))

        def sem(name):
            return ctx.enter_context(nc.semaphore(name))

        ring = [sb(f"ring{i}", [P, CHUNK]) for i in range(RING)]
        hT = sb("hT", [P, KT, T])
        xnT = sb("xnT", [P, KT, T])
        bias = sb("bias", [P, HEADS, BAND])
        areaA = sb("areaA", [P, KT * T])
        areaB = sb("areaB", [P, KT * T])
        areaK = sb("areaK", [P, KT * T])
        lru = sb("lru", [P, KT, CONV - 1 + T])
        gate_a = sb("gate_a", [P, KT, T])
        gate_b = sb("gate_b", [P, KT, T])
        v_sb = sb("v_sb", [P, TT, KV_HEADS * HD])
        p_sb = sb("p_sb", [P, DEPTH, PLE // P, T])
        wrg = sb("wrg", [P, KT, HD])
        wig = sb("wig", [P, KT, HD])
        ident = sb("ident", [P, P])
        ones = sb("ones", [P, P])
        flip = sb("flip", [P, P])
        NCOL = cols.shape[1]
        col = sb("col", [P, NCOL, KT])
        NROW = rows.shape[1]
        row = sb("row", [P, NROW])
        rel = sb("rel", [HEADS, BUCKETS])
        decay = sb("decay", [P, 3, DEPTH, KT])
        small = sb("small", [P, 96])

        q_tok = areaA[:, :].rearrange("p (t n) -> p t n", t=TT)
        yaT = areaA[:, :].rearrange("p (k t) -> p k t", k=KT)
        glgT = yaT
        qT = areaB[:, :].rearrange("p (k t) -> p k t", k=KT)
        decayT = qT
        k_dup = areaK[:, 0:1024].rearrange("p (t g s d) -> p t g s d", t=TT, g=KV_HEADS, s=2)
        k_dup2 = areaK[:, 0:1024].rearrange("p (t g n) -> p t g n", t=TT, g=KV_HEADS)
        kTT = areaK[:, 1024:2048].rearrange("p (g t) -> p g t", g=KV_HEADS)
        rT = areaK[:, :].rearrange("p (k t) -> p k t", k=KT)
        rms = areaB[:, 0:T]
        rinv = areaB[:, T:2 * T]
        spare = ring[RING - 1]
        xcT = spare[:, 0:2048].rearrange("p (k t) -> p k t", k=KT)
        ebuf = spare[:, 2048:3072].rearrange("p (b h s) -> p b h s", b=2, h=2)
        ptb = spare[:, 3072:4096].rearrange("p (b h s) -> p b h s", b=2, h=2)
        sqs = spare[:, 2048:3072].rearrange("p (b n) -> p b n", b=2)
        band = spare[:, :].rearrange("p (h s) -> p h s", h=HEADS)
        u_line = gate_a[0:HEADS, 0, :]
        u_line = gate_a[:, :, :].rearrange("p k t -> p (k t)")[0:HEADS, 0:U_LEN]
        u_zero = gate_a[:, :, :].rearrange("p k t -> p (k t)")[0:HEADS, U_LEN:U_LEN + P]

        work = [ctx.enter_context(nc.psum_tensor(f"work{i}", [P, 512], F32)) for i in range(2)]
        acc = [ctx.enter_context(nc.psum_tensor(f"acc{i}", [P, 1024], F32)) for i in range(2)]
        pv_ps = ctx.enter_context(nc.psum_tensor("pv_ps", [P, 512], F32))
        misc = ctx.enter_context(nc.psum_tensor("misc", [P, 512], F32))
        quad = [acc[0][:, 0:512], acc[0][:, 512:1024], acc[1][:, 0:512], acc[1][:, 512:1024]]

        score_ps = acc[0][:, :].rearrange("p (h s) -> p h s", h=2)

        slot_full = [sem(f"slot_full{i}") for i in range(RING)]
        slot_free = [sem(f"slot_free{i}") for i in range(RING)]
        work_full = [sem(f"work_full{i}") for i in range(2)]
        work_free = [sem(f"work_free{i}") for i in range(2)]
        x_in = sem("x_in")
        small_in = sem("small_in")
        p_in = sem("p_in")
        rel_in = sem("rel_in")
        gates_in = sem("gates_in")
        line_out = sem("line_out")
        band_in = sem("band_in")
        consts = sem("consts")
        ident_ok = sem("ident_ok")
        line_ok = sem("line_ok")
        flipped = sem("flipped")
        bias_ok = sem("bias_ok")
        exp_lam = sem("exp_lam")
        abs_lam = sem("abs_lam")
        dve_step = sem("dve_step")
        pool_step = sem("pool_step")
        squared = sem("squared")
        summed = sem("summed")
        rooted = sem("rooted")
        normed = sem("normed")
        h_mixed = sem("h_mixed")
        h_ffn = sem("h_ffn")
        h_ple = sem("h_ple")
        qk_squared = sem("qk_squared")
        qk_summed = sem("qk_summed")
        qk_rooted = sem("qk_rooted")
        qk_normed = sem("qk_normed")
        qk_turned = sem("qk_turned")
        qkT_ok = sem("qkT_ok")
        scored = sem("scored")
        biased = sem("biased")
        max_ok = sem("max_ok")
        exped = sem("exped")
        probs_ok = sem("probs_ok")
        probs_turned = sem("probs_turned")
        probsT_ok = sem("probsT_ok")
        pv_done = sem("pv_done")
        pv_taken = sem("pv_taken")
        conv_done = sem("conv_done")
        ri_done = sem("ri_done")
        sig_ga = sem("sig_ga")
        sig_ri = sem("sig_ri")
        sig_gb = sem("sig_gb")
        decay_ok = sem("decay_ok")
        tanh_ok = sem("tanh_ok")
        sqrt_ok = sem("sqrt_ok")
        lg_ok = sem("lg_ok")
        yb_ok = sem("yb_ok")
        merged = sem("merged")
        silu_ok = sem("silu_ok")
        hid_ok = sem("hid_ok")
        ffn_acc = sem("ffn_acc")
        ple_gate = sem("ple_gate")
        out_done = sem("out_done")

        xn_tok = q_tok
        xg = areaB[:, :].rearrange("p (s k n) -> p s k n", s=2, k=KT)
        y_sb = areaK[:, :].rearrange("p (s n) -> p s n", s=2)
        scr = lru[:, :, :].rearrange("p k t -> p (k t)")
        m_silu = scr[:, 0:512]
        m_hid = [scr[:, 512:1024], scr[:, 1024:1536]]
        m_hidT = scr[:, 1536:2048].rearrange("p (f n) -> p f n", f=FT)
        gbf = gate_b[:, :, :].rearrange("p k t -> p (k t)")
        m_pick = gbf[:, 0:512].rearrange("p (t n) -> p t n", t=TT)
        m_gpick = gbf[:, 512:1024].rearrange("p (t n) -> p t n", t=TT)
        m_gpickT = gbf[:, 1024:1536].rearrange("p (s t) -> p s t", s=2)
        iota_f = gbf[:, 1536:1792]
        gaf = gate_a[:, :, :].rearrange("p k t -> p (k t)")
        before = gaf[:, 0:P]
        iota_i = gaf[:, 512:768].bitcast(I32)
        route = gaf[:, 1024:1280].rearrange("p (n t e) -> p n t e", n=16, t=TT)
        rank_m = gaf[:, 1536:1568].rearrange("p (t e) -> p t e", t=TT)
        gate_m = gaf[:, 1568:1600].rearrange("p (t e) -> p t e", t=TT)
        pick_w = gaf[:, 1600:1608]
        pick_wi = gaf[:, 1608:1616].bitcast(I32)
        counts = gaf[:, 1616:1624].bitcast(I32)
        rw = sb("rw", [P, KT, EXPERTS])
        rsmall = gaf[:, 1632:1664].rearrange("p (n t) -> p n t", t=TT)

        logits_done = sem("logits_done")
        tok_turned = sem("tok_turned")
        tok_ok = sem("tok_ok")
        route_masks = sem("route_masks")
        route_diff = sem("route_diff")
        route_exp = sem("route_exp")
        ranked = sem("ranked")
        counts_ok = sem("counts_ok")
        pool_route = sem("pool_route")
        m_full = [sem(f"m_full{i}") for i in range(2)]
        m_taken = [sem(f"m_taken{i}") for i in range(2)]
        m_built = sem("m_built")
        m_gturned = sem("m_gturned")
        m_gtaken = sem("m_gtaken")
        m_turned = sem("m_turned")
        m_turn_taken = sem("m_turn_taken")
        m_y = sem("m_y")
        m_y_taken = sem("m_y_taken")
        m_combined = sem("m_combined")
        m_added = sem("m_added")
        m_down = sem("m_down")
        M_MASK = 6
        hid = areaA[:, :].rearrange("p (b f t) -> p b f t", b=2, f=FT)

        C_MIX, C_FFN, C_PLE, C_CONV, C_CB, C_RG, C_IG, C_LAM = (
            0, DEPTH, 2 * DEPTH, 3 * DEPTH, 7 * DEPTH, 8 * DEPTH, 9 * DEPTH, 10 * DEPTH)
        R_Q, R_K, R_SINK, R_RB = 0, DEPTH * HD, 2 * DEPTH * HD, 2 * DEPTH * HD + DEPTH * HEADS

        def chunk(key, k):
            return ring[at[key][0]][:, :].rearrange("p (k n) -> p k n", k=k)

        def bank_of(l, *g):
            b, _ = place[(l, *g)]
            return work[b]

        def taken(ins, l, *g):
            ins.then_inc(work_free[place[(l, *g)][0]], 1)

        def wait_full(eng, l, *g):
            b, n = place[(l, *g)]
            eng.wait_ge(work_full[b], n + 1)

        def wait_h(eng, n):
            l, part = divmod(n, 3)
            if part == 0 and l == 0:
                eng.wait_ge(x_in, 16)
            elif part == 0:
                eng.wait_ge(h_ple, KT * l)
            elif part == 1:
                eng.wait_ge(h_mixed, KT * (l + 1))
            elif l % 2 == 0:
                eng.wait_ge(h_ffn, 4 * (l // 2 + 1))
            else:
                eng.wait_ge(m_added, 1 + 8 * EXPERTS)

        quads6 = [quad[0], quad[1], quad[2], quad[3], pv_ps[:, :], misc[:, :]]
        FIRST_UNIT = 4
        UNITS = TT * PAIRS
        silu_buf = areaB[:, 1024:1536].rearrange("p (b t) -> p b t", b=2)

        block = ctx.enter_context(nc.Block())

        @block.sync
        def _(sp):
            def load(key, src):
                slot, use = at[key]
                if use:
                    sp.wait_ge(slot_free[slot], use)
                sp.dma_start(ring[slot][:, 0:src.shape[1]], src).then_inc(slot_full[slot], 16)

            sp.dma_start(hT[:, :, :], xT).then_inc(x_in, 16)
            for l in range(DEPTH):
                if l:
                    sp.wait_ge(ri_done, KT * l)
                sp.dma_start(wrg[:, :, :], wrg_d[l]).then_inc(gates_in, 16)
                sp.dma_start(wig[:, :, :], wig_d[l]).then_inc(gates_in, 16)
                for i in range(MIX_CHUNKS):
                    load((l, "mix", i), mix_w[l, i])
                if l % 2 == 0:
                    for i, (w, c) in enumerate(ffn_order()):
                        if i == RING - 1:
                            wait_full(sp, l, "pb", KT - 1)
                        load((l, w, c), dense_w[i])
                else:
                    with sp.Fori(0, EXPERTS) as e:
                        for i in range(FFN_CHUNKS):
                            slot, turn = i % RING, i // RING
                            if i == RING - 1:
                                wait_full(sp, l, "pb", KT - 1)
                            sp.wait_ge(slot_free[slot], e * (FFN_CHUNKS // RING) + (moe_base[slot] + turn))
                            sp.dma_start(ring[slot][:, :], moe_w[e, i]).then_inc(slot_full[slot], 16)
                for i in range(PLE_CHUNKS):
                    load((l, "ple", i), ple_w[l, i])
                load((l, "ple", PLE_CHUNKS), ple_p[l])
            sp.wait_ge(h_ple, KT * DEPTH)
            sp.dma_start(outT, hT[:, :, :]).then_inc(out_done, 16)
            sp.wait_ge(out_done, 16)

        @block.gpsimd
        def _(pool):
            pool.memset(ident[:, :], 0.0).then_inc(pool_step, 1)
            pool.memset(flip[:, :], 0.0).then_inc(pool_step, 1)
            pool.memset(ones[:, :], 1.0).then_inc(consts, 1)
            pool.wait_ge(pool_step, 2)
            pool.affine_select(out=flip[:, :], in_=flip[:, :], compare_op=ALU.not_equal, fill=1.0,
                               base=-(P - 1), pattern=[[1, P]], channel_multiplier=1).then_inc(consts, 1)
            pool.affine_select(out=ident[:, :], in_=ident[:, :], compare_op=ALU.not_equal, fill=1.0,
                               base=0, pattern=[[-1, P]], channel_multiplier=1).then_inc(ident_ok, 1)
            pool.wait_ge(h_mixed, KT * DEPTH)
            pool.memset(before, 1.0).then_inc(pool_step, 1)
            pool.iota(iota_i, pattern=[[1, 2 * P]], base=0, channel_multiplier=0).then_inc(pool_step, 1)
            pool.iota(pick_wi, pattern=[[-1, EXPERTS]], base=EXPERTS, channel_multiplier=0).then_inc(pool_step, 1)
            pool.wait_ge(pool_step, 5)
            pool.affine_select(out=before, in_=before, compare_op=ALU.is_gt, fill=0.0,
                               base=0, pattern=[[1, P]], channel_multiplier=-1).then_inc(pool_route, 1)
            pool.tensor_copy(iota_f, iota_i).then_inc(pool_route, 1)
            pool.tensor_copy(pick_w, pick_wi).then_inc(pool_route, 1)

        @block.scalar
        def _(act):
            act.dma_start(rel[:, :], relT).then_inc(rel_in, 16)
            act.dma_start(col[:, :, :], cols).then_inc(small_in, 16)
            act.dma_start(row[:, :], rows).then_inc(small_in, 16)
            act.dma_start(rw[:, :, :], router_d).then_inc(small_in, 16)
            act.dma_start(p_sb[:, :, :, :], pT).then_inc(p_in, 16)
            act.wait_ge(line_ok, 1)
            act.dma_start(bias_line.ap(), u_line).then_inc(line_out, 16)
            act.wait_ge(line_out, 16)
            act.dma_start(band, bass.AP(bias_line, 0, [[1, P], [U_LEN, HEADS], [1, BAND]])).then_inc(band_in, 16)

            act.wait_ge(abs_lam, 1)
            act.activation(decay[:, 1, :, :], decay[:, 0, :, :], ACT.Exp, scale=-1.0).then_inc(exp_lam, 1)

            def norm(n):
                wait_h(act, n)
                for q in range(4):
                    act.activation(xnT[:, 2 * q:2 * q + 2, :], hT[:, 2 * q:2 * q + 2, :], ACT.Square).then_inc(squared, 1)
                act.wait_ge(summed, n + 1)
                act.activation(rms, misc[:, 0:T], ACT.Sqrt, bias=eps_col[:, 0:1], scale=1.0 / D).then_inc(rooted, 1)

            eps_col = small[:, 64:65]

            def qk_norm(l):
                for i in range(6):
                    c, tt = i // 2, i % 2
                    n = 512 if c < 2 else 256
                    wait_full(act, l, "qkv", c, tt)
                    if i >= 2:
                        act.wait_ge(qk_summed, 6 * l + i - 1)
                    if c == 2:
                        act.activation(v_sb[:, tt, :], work[place[(l, "qkv", c, tt)][0]][:, 256:512], ACT.Copy)
                    act.activation(sqs[:, i % 2, 0:n], bank_of(l, "qkv", c, tt)[:, 0:n], ACT.Square).then_inc(qk_squared, 1)
                    act.wait_ge(qk_summed, 6 * l + i + 1)
                    act.activation(small[:, 8 * (i % 2) + 16:8 * (i % 2) + 16 + n // HD],
                                   small[:, 8 * (i % 2):8 * (i % 2) + n // HD],
                                   ACT.Sqrt, bias=eps_col, scale=1.0 / HD).then_inc(qk_rooted, 1)

            def qk_turns(l):
                for i in range(6):
                    act.wait_ge(qk_turned, 6 * l + i + 1)
                    src = quads6[i].rearrange("p (j n) -> p j n", j=4)
                    if i < 4:
                        c, tt = i // 2, i % 2
                        dst = qT[:, 4 * c:4 * c + 4, tt * P:(tt + 1) * P]
                    else:
                        dst = kTT[:, :, (i - 4) * P:(i - 3) * P]
                    act.activation(dst, src, ACT.Copy).then_inc(qkT_ok, 1)

            def evacuate(l, name, j, dst):
                wait_full(act, l, name, j)
                taken(act.activation(dst, bank_of(l, name, j)[:, 0:T], ACT.Copy), l, name, j)

            def exps(l, u):
                g = PAIRS * TT * l + u
                b, t = divmod(u, PAIRS)
                w = P * (b + 1)
                act.wait_ge(max_ok, g + 1)
                m = 32 + 8 * (u % 2)
                for hh in range(2):
                    e = ebuf[:, u % 2, hh, 0:w]
                    act.activation(e, e, ACT.Exp, bias=small[:, m + 2 + hh:m + 3 + hh],
                                   accum_out=small[:, m + 6 + hh:m + 7 + hh])
                act.activation(small[:, m + 4:m + 6], small[:, m + 4:m + 6], ACT.Exp).then_inc(exped, 1)

            def probsT(l, u):
                g = PAIRS * TT * l + u
                w = P * (u // PAIRS + 1)
                act.wait_ge(probs_turned, g + 1)
                if u >= 2:
                    act.wait_ge(pv_done, g - 1)
                act.activation(ptb[:, u % 2, :, 0:w],
                               acc[1][:, 512 * (u % 2):512 * (u % 2) + 512].rearrange("p (h s) -> p h s", h=2)[:, :, 0:w],
                               ACT.Copy).then_inc(probsT_ok, 1)

            def take_pv(l, u):
                g = PAIRS * TT * l + u
                b, t = divmod(u, PAIRS)
                act.wait_ge(pv_done, g + 1)
                act.activation(yaT[:, t, b * P:(b + 1) * P], (pv_ps, misc)[u % 2][:, 0:P],
                               ACT.Copy).then_inc(pv_taken, 1)

            def gates(l):
                act.wait_ge(work_free[place[(l, "ga", KT - 1)][0]], place[(l, "ga", KT - 1)][1] + 1)
                act.wait_ge(work_free[place[(l, "ga", KT - 2)][0]], place[(l, "ga", KT - 2)][1] + 1)
                act.activation(gate_a[:, :, :], gate_a[:, :, :], ACT.Sigmoid).then_inc(sig_ga, 1)
                for c in range(KT):
                    act.wait_ge(ri_done, KT * l + c + 1)
                    act.activation(rT[:, c, :], quad[c % 4][:, 0:T], ACT.Sigmoid, bias=col[:, C_RG + l, c:c + 1])
                    act.activation(lru[:, c, CONV - 1:], quad[c % 4][:, T:2 * T], ACT.Sigmoid,
                                   bias=col[:, C_IG + l, c:c + 1]).then_inc(sig_ri, 1)
                act.activation(gate_b[:, :, :], gate_b[:, :, :], ACT.Sigmoid).then_inc(sig_gb, 1)
                for c in range(KT):
                    act.wait_ge(sig_ri, KT * l + c + 1)
                    act.activation(decayT[:, c, :], rT[:, c, :], ACT.Exp, scale=decay[:, 1, l, c:c + 1]).then_inc(decay_ok, 1)
                    act.activation(rT[:, c, :], rT[:, c, :], ACT.Tanh, scale=decay[:, 2, l, c:c + 1]).then_inc(tanh_ok, 1)
                for c in range(KT):
                    act.wait_ge(tanh_ok, KT * l + c + 1)
                    act.activation(rT[:, c, :], rT[:, c, :], ACT.Sqrt).then_inc(sqrt_ok, 1)

            def mixer(l):
                qk_norm(l)
                order = [("lx", j) for j in range(KT)] + [("gb", j) for j in range(KT)] + [("ga", j) for j in range(KT)]
                for g, (name, j) in enumerate(order):
                    dst = {"lx": lru[:, j, CONV - 1:], "gb": gate_b[:, j, :], "ga": gate_a[:, j, :]}[name]
                    evacuate(l, name, j, dst)
                    s = g - FIRST_UNIT
                    if g == FIRST_UNIT - 1:
                        qk_turns(l)
                    if 0 <= s - 2 < UNITS:
                        probsT(l, s - 2)
                    if 0 <= s - 3 < UNITS:
                        take_pv(l, s - 3)
                    if 0 <= s < UNITS:
                        exps(l, s)
                gates(l)
                for j in range(KT):
                    wait_full(act, l, "lg", j)
                    ins = act.activation(glgT[:, j, :], bank_of(l, "lg", j)[:, 0:T], ACT.Gelu_apprx_tanh)
                    taken(ins, l, "lg", j)

            def dense(l):
                for i in range(FC * FT):
                    c, ft = divmod(i, FT)
                    wait_full(act, l, "ffn", c, ft)
                    if i >= 2:
                        act.wait_ge(hid_ok, FC * FT * (l // 2) + i - 1)
                    act.activation(silu_buf[:, i % 2, :], bank_of(l, "ffn", c, ft)[:, 0:T], ACT.Silu).then_inc(silu_ok, 1)

            def ple(l):
                for j in range(KT):
                    wait_full(act, l, "ple", j)
                    if j >= 2:
                        act.wait_ge(h_ple, KT * l + j - 1)
                    act.activation(silu_buf[:, j % 2, :], bank_of(l, "ple", j)[:, 0:T], ACT.Sigmoid).then_inc(ple_gate, 1)

            def expert(tiles, e):
                w = 2 // tiles
                for st in range(tiles):
                    act.wait_ge(m_full[0], e * 16 + w * (st + 1))
                    act.activation(xg[:, st, 0:4, :], work[0][:, :].rearrange("p (k n) -> p k n", k=4), ACT.Copy).then_inc(m_taken[0], w)
                    act.wait_ge(m_gturned, e * 2 + w * (st + 1))
                    act.activation(m_gpickT[:, st, :], misc[:, 0:T], ACT.Copy).then_inc(m_gtaken, w)

                def turn(it):
                    act.wait_ge(m_turned, e * 14 + w * (it + 1))
                    act.activation(m_hidT, pv_ps[:, :].rearrange("p (f n) -> p f n", f=FT), ACT.Copy).then_inc(m_turn_taken, w)

                for c in range(FC + 1):
                    for st in range(tiles):
                        it = c * tiles + st
                        if c < FC:
                            act.wait_ge(m_full[0], e * 16 + w * (tiles + it + 1))
                            act.wait_ge(m_taken[1], e * 16 + (1 + w * (tiles + it)))
                            act.activation(m_silu, work[0][:, :], ACT.Silu).then_inc(m_taken[0], w)
                        if c:
                            turn(it - tiles)
                for st in range(tiles):
                    act.wait_ge(m_y, e * 2 + w * (st + 1))
                    act.activation(y_sb[:, st, :], acc[st][:, :], ACT.Copy).then_inc(m_y_taken, w)

            def moe(l):
                for i in range(4):
                    act.wait_ge(tok_turned, i + 1)
                    tt, half = divmod(i, 2)
                    act.activation(xn_tok[:, tt, half * 512:(half + 1) * 512], quad[i], ACT.Copy).then_inc(tok_ok, 1)
                act.wait_ge(route_diff, 1)
                act.activation(rsmall[:, 3, :], rsmall[:, 2, :], ACT.Exp).then_inc(route_exp, 1)
                act.wait_ge(counts_ok, 1)
                act.sem_inc(m_taken[0], 1)
                act.sem_inc(m_y_taken, 1)
                with act.Fori(0, EXPERTS) as e:
                    n = act.value_load(counts[0:1, bass.ds(e, 1)], min_val=0, max_val=T)
                    with act.If(n <= P):
                        expert(1, e)
                    with act.Else():
                        expert(2, e)

            norm(0)
            for i in range(8):
                act.wait_ge(flipped, i + 1)
                act.activation(bias[:, 2 * i:2 * i + 2, :], quad[i % 4].rearrange("p (h s) -> p h s", h=2), ACT.Copy).then_inc(bias_ok, 1)
            for l in range(DEPTH):
                if l:
                    norm(3 * l)
                mixer(l)
                norm(3 * l + 1)
                dense(l) if l % 2 == 0 else moe(l)
                norm(3 * l + 2)
                ple(l)

        @block.tensor
        def _(pe):
            def group_open(l, *g):
                b, n = place[(l, *g)]
                if n:
                    pe.wait_ge(work_free[b], n)
                return work[b]

            def group_close(ins, l, *g):
                ins.then_inc(work_full[place[(l, *g)][0]], 1)

            def need(key):
                slot, use = at[key]
                pe.wait_ge(slot_full[slot], 16 * (use + 1))

            def release(ins_sem_owner, key):
                pe.sem_inc(slot_free[at[key][0]], 1)

            def norm(n):
                for k in range(KT):
                    if k % 2 == 0:
                        pe.wait_ge(squared, 4 * n + k // 2 + 1)
                    mm = pe.matmul(misc[:, 0:T], ones[:, :], xnT[:, k, :], start=(k == 0), stop=(k == KT - 1))
                mm.then_inc(summed, 1)

            def product(l, name, j, key, src, wait_src=None):
                w = chunk(key, KT)
                if j % FT == 0:
                    need(key)
                out = group_open(l, name, j)
                for k in range(KT):
                    if wait_src is not None:
                        wait_src(k)
                    mm = pe.matmul(out[:, 0:T], w[:, k, (j % FT) * P:(j % FT + 1) * P], src[:, k, :],
                                   start=(k == 0), stop=(k == KT - 1))
                group_close(mm, l, name, j)
                if j % FT == FT - 1:
                    wait_full(pe, l, name, j)
                    release(None, key)

            def qkv(l):
                for c in range(3):
                    need((l, "mix", c))
                    w = chunk((l, "mix", c), KT)
                    for tt in range(TT):
                        out = group_open(l, "qkv", c, tt)
                        for k in range(KT):
                            if c == 0 and tt == 0:
                                pe.wait_ge(normed, KT * 3 * l + k + 1)
                            mm = pe.matmul(out[:, :], xnT[:, k, tt * P:(tt + 1) * P], w[:, k, :],
                                           start=(k == 0), stop=(k == KT - 1))
                        group_close(mm, l, "qkv", c, tt)
                    wait_full(pe, l, "qkv", c, TT - 1)
                    release(None, (l, "mix", c))

            def turn_qk(l):
                for i in range(6):
                    pe.wait_ge(qk_normed, 6 * l + i + 1)
                    for j in range(4):
                        if i < 4:
                            c, tt = i // 2, i % 2
                            src = q_tok[:, tt, (4 * c + j) * P:(4 * c + j + 1) * P]
                        else:
                            src = k_dup2[:, i - 4, j, :]
                        mm = pe.transpose(quads6[i][:, j * P:(j + 1) * P], src, ident[:, :])
                    mm.then_inc(qk_turned, 1)

            def scores(l, u):
                g = UNITS * l + u
                b, t = divmod(u, PAIRS)
                w = P * (b + 1)
                if u == 0:
                    pe.wait_ge(qkT_ok, 6 * (l + 1))
                if u:
                    pe.wait_ge(biased, g)
                for hh in range(2):
                    mm = pe.matmul(score_ps[:, hh, 0:w],
                                   qT[HD * hh:HD * hh + HD, t, b * P:(b + 1) * P],
                                   kTT[HD * hh:HD * hh + HD, t // 2, 0:w], start=True, stop=True)
                mm.then_inc(scored, 1)

            def turn_probs(l, u):
                g = UNITS * l + u
                pe.wait_ge(probs_ok, g + 1)
                if u >= 2:
                    pe.wait_ge(probsT_ok, g - 1)
                for hh in range(2):
                    for kt in range(u // PAIRS + 1):
                        o = 512 * (u % 2) + BAND * hh + P * kt
                        mm = pe.transpose(acc[1][:, o:o + P], ebuf[:, u % 2, hh, P * kt:P * kt + P], ident[:, :])
                mm.then_inc(probs_turned, 1)

            def values(l, u):
                g = UNITS * l + u
                b, t = divmod(u, PAIRS)
                kv = t // 2
                pe.wait_ge(probsT_ok, g + 1)
                if u >= 2:
                    pe.wait_ge(pv_taken, g - 1)
                for hh in range(2):
                    for kt in range(b + 1):
                        mm = pe.matmul((pv_ps, misc)[u % 2][HD * hh:HD * hh + HD, 0:P],
                                       v_sb[:, kt, kv * HD:(kv + 1) * HD], ptb[:, u % 2, hh, P * kt:P * kt + P],
                                       start=(kt == 0), stop=(kt == b))
                mm.then_inc(pv_done, 1)

            def recurrence_gates(l):
                pe.wait_ge(gates_in, 32 * (l + 1))
                for c in range(KT):
                    pe.wait_ge(conv_done, KT * l + c + 1)
                    if c >= 4:
                        pe.wait_ge(sig_ri, KT * l + c - 3)
                    for n, w in enumerate((wrg, wig)):
                        for b in range(2):
                            mm = pe.matmul(quad[c % 4][HD * b:HD * b + HD, T * n:T * n + T],
                                           w[HD * b:HD * b + HD, c, :], xcT[HD * b:HD * b + HD, c, :],
                                           start=True, stop=True)
                    mm.then_inc(ri_done, 1)

            def mixer(l):
                qkv(l)
                order = [("lx", j, 3) for j in range(KT)] + [("gb", j, 5) for j in range(KT)] + [("ga", j, 7) for j in range(KT)]
                for g, (name, j, first) in enumerate(order):
                    product(l, name, j, (l, "mix", first + j // FT), xnT)
                    s = g - FIRST_UNIT
                    if g == FIRST_UNIT - 1:
                        turn_qk(l)
                    if 0 <= s < UNITS:
                        scores(l, s)
                    if 0 <= s - 2 < UNITS:
                        turn_probs(l, s - 2)
                    if 0 <= s - 3 < UNITS:
                        values(l, s - 3)
                recurrence_gates(l)
                pe.wait_ge(pv_taken, UNITS * (l + 1))
                for j in range(KT):
                    product(l, "pa", j, (l, "mix", 9 + j // FT), yaT)
                for j in range(KT):
                    product(l, "lg", j, (l, "mix", 11 + j // FT), xnT)
                for j in range(KT):
                    product(l, "pb", j, (l, "mix", 13 + j // FT), xcT,
                            (lambda k: pe.wait_ge(yb_ok, KT * l + k + 1)) if j == 0 else None)
                for j in range(KT):
                    product(l, "out", j, (l, "mix", 15 + j // FT), gate_a,
                            (lambda k: pe.wait_ge(merged, KT * l + k + 1)) if j == 0 else None)

            def dense(l):
                pe.wait_ge(normed, KT * (3 * l + 2))

                def down(c):
                    need((l, "w2", c))
                    w = chunk((l, "w2", c), FT)
                    pe.wait_ge(hid_ok, FC * FT * (l // 2) + FT * (c + 1))
                    for ft in range(FT):
                        for j in range(KT):
                            mm = pe.matmul(quad[j // 2][:, T * (j % 2):T * (j % 2) + T],
                                           w[:, ft, j * P:(j + 1) * P], hid[:, c % 2, ft, :],
                                           start=(c == 0 and ft == 0 and j % 2 == 0),
                                           stop=(c == FC - 1 and ft == FT - 1), skip_group_check=True)
                    mm.then_inc(ffn_acc, 1)
                    pe.wait_ge(ffn_acc, FC * (l // 2) + c + 1)
                    release(None, (l, "w2", c))

                for c in range(FC):
                    need((l, "w1", c))
                    need((l, "w3", c))
                    for ft in range(FT):
                        out = group_open(l, "ffn", c, ft)
                        for half, w in enumerate(("w1", "w3")):
                            wt = chunk((l, w, c), KT)
                            for k in range(KT):
                                mm = pe.matmul(out[:, T * half:T * half + T], wt[:, k, ft * P:(ft + 1) * P],
                                               xnT[:, k, :], start=(k == 0), stop=(k == KT - 1))
                        group_close(mm, l, "ffn", c, ft)
                    wait_full(pe, l, "ffn", c, FT - 1)
                    release(None, (l, "w1", c))
                    release(None, (l, "w3", c))
                    if c:
                        down(c - 1)
                down(FC - 1)

            def ple(l):
                n = 3 * l + 2
                pe.wait_ge(normed, KT * (n + 1))
                pe.wait_ge(p_in, 16)
                for j in range(KT):
                    key = (l, "ple", j // FT)
                    if j % FT == 0:
                        need(key)
                    if j == 0:
                        need((l, "ple", PLE_CHUNKS))
                    out = group_open(l, "ple", j)
                    w = chunk(key, KT)
                    for k in range(KT):
                        pe.matmul(out[:, 0:T], w[:, k, (j % FT) * P:(j % FT + 1) * P], xnT[:, k, :],
                                  start=(k == 0), stop=(k == KT - 1))
                    wp = ring[at[(l, "ple", PLE_CHUNKS)][0]][:, 0:2048].rearrange("p (k n) -> p k n", k=2)
                    for k in range(2):
                        mm = pe.matmul(out[:, T:2 * T], wp[:, k, j * P:(j + 1) * P], p_sb[:, l, k, :],
                                       start=(k == 0), stop=(k == 1))
                    group_close(mm, l, "ple", j)
                    if j % FT == FT - 1:
                        wait_full(pe, l, "ple", j)
                        release(None, key)
                release(None, (l, "ple", PLE_CHUNKS))

            def expert(tiles, e):
                w = 2 // tiles

                def chunk_at(key):
                    i = FFN_AT[key]
                    slot, turn = i % RING, i // RING
                    return slot, moe_base[slot] + turn

                def need_e(key):
                    slot, use = chunk_at(key)
                    pe.wait_ge(slot_full[slot], e * (16 * (FFN_CHUNKS // RING)) + 16 * (use + 1))

                for st in range(tiles):
                    if st == 0:
                        pe.wait_ge(m_built, e + 1)
                    for half in range(2):
                        pe.wait_ge(m_taken[half], e * 16 + (1 + w * st))
                        for kk in range(4):
                            k = 4 * half + kk
                            for tt in range(TT):
                                mm = pe.matmul(work[half][:, kk * P:(kk + 1) * P], xn_tok[:, tt, k * P:(k + 1) * P],
                                               m_pick[:, tt, st * P:(st + 1) * P],
                                               start=(tt == 0), stop=(tt == TT - 1))
                        mm.then_inc(m_full[half], w)
                    if st == 0:
                        pe.wait_ge(m_added, e * 8 + 1)
                    else:
                        pe.wait_ge(m_gtaken, e * 2 + w * st)
                    for tt in range(TT):
                        mm = pe.transpose(misc[:, tt * P:(tt + 1) * P], m_gpick[:, tt, st * P:(st + 1) * P], ident[:, :])
                    mm.then_inc(m_gturned, w)

                def up(half, c, st):
                    name = ("w1", "w3")[half]
                    it = c * tiles + st
                    if st == 0:
                        need_e((name, c))
                    pe.wait_ge(m_taken[half], e * 16 + (1 + w * (tiles + it)))
                    if half == 0 and it == 0:
                        pe.wait_ge(m_taken[1], e * 16 + (1 + w * tiles))
                    wt = ring[chunk_at((name, c))[0]][:, :].rearrange("p (k n) -> p k n", k=KT)
                    for k in range(KT):
                        mm = pe.matmul(work[half][:, :], xg[:, st, k, :], wt[:, k, :], start=(k == 0), stop=(k == KT - 1))
                    mm.then_inc(m_full[half], w)
                    if st == tiles - 1:
                        pe.wait_ge(m_full[half], e * 16 + w * (tiles + it + 1))
                        pe.sem_inc(slot_free[chunk_at((name, c))[0]], 1)

                def turn(c, st):
                    it = c * tiles + st
                    pe.wait_ge(m_taken[1], e * 16 + (1 + w * (tiles + it + 1)))
                    if it:
                        pe.wait_ge(m_turn_taken, e * 14 + w * it)
                    for ft in range(FT):
                        mm = pe.transpose(pv_ps[:, ft * P:(ft + 1) * P], m_hid[st][:, ft * P:(ft + 1) * P], ident[:, :])
                    mm.then_inc(m_turned, w)

                def down(c, st):
                    it = c * tiles + st
                    if st == 0:
                        need_e(("w2", c))
                    pe.wait_ge(m_turn_taken, e * 14 + w * (it + 1))
                    if c == 0:
                        pe.wait_ge(m_y_taken, e * 2 + 1)
                    wt = ring[chunk_at(("w2", c))[0]][:, :].rearrange("p (f n) -> p f n", f=FT)
                    for ft in range(FT):
                        for half in range(2):
                            mm = pe.matmul(acc[st][:, 512 * half:512 * half + 512], m_hidT[:, ft, :],
                                           wt[:, ft, 512 * half:512 * half + 512],
                                           start=(c == 0 and ft == 0), stop=(c == FC - 1 and ft == FT - 1))
                    mm.then_inc(m_down, w)
                    if c == FC - 1:
                        pass
                    if st == tiles - 1:
                        pe.wait_ge(m_down, e * 14 + w * (it + 1))
                        pe.sem_inc(slot_free[chunk_at(("w2", c))[0]], 1)

                for c in range(FC + 1):
                    for st in range(tiles):
                        if c < FC:
                            up(0, c, st)
                        if c:
                            turn(c - 1, st)
                        if c < FC:
                            up(1, c, st)
                        if c:
                            down(c - 1, st)
                pe.sem_inc(m_y, 2)
                pe.wait_ge(m_gtaken, e * 2 + 2)
                for st in range(tiles):
                    pe.wait_ge(m_y_taken, e * 2 + (1 + w * (st + 1)))
                    for q in range(4):
                        i = 4 * st + q
                        if i >= 2:
                            pe.wait_ge(m_added, e * 8 + (1 + w * (i - 1)))
                        for kk in range(2):
                            k = 2 * q + kk
                            mm = pe.matmul((pv_ps, misc)[q % 2][:, T * kk:T * kk + T], y_sb[:, st, k * P:(k + 1) * P],
                                           m_gpickT[:, st, :], start=True, stop=True)
                        mm.then_inc(m_combined, w)

            def moe(l):
                pe.wait_ge(normed, KT * (3 * l + 2))
                for tt in range(TT):
                    for k in range(KT):
                        mm = pe.matmul(misc[:, 8 * tt:8 * tt + 8], xnT[:, k, tt * P:(tt + 1) * P], rw[:, k, :],
                                       start=(k == 0), stop=(k == KT - 1))
                mm.then_inc(logits_done, 1)
                for i in range(4):
                    tt, half = divmod(i, 2)
                    for kk in range(4):
                        mm = pe.transpose(quad[i][:, kk * P:(kk + 1) * P],
                                          xnT[:, 4 * half + kk, tt * P:(tt + 1) * P], ident[:, :])
                    mm.then_inc(tok_turned, 1)
                pe.wait_ge(route_masks, 1)
                pe.wait_ge(pool_route, 3)
                mk = route[:, M_MASK, :, :]
                pe.matmul(misc[:, 64:72], before, mk[:, 0, :], start=True, stop=True)
                pe.matmul(misc[:, 72:80], ones[:, :], mk[:, 0, :], start=True, stop=False)
                pe.matmul(misc[:, 72:80], before, mk[:, 1, :], start=False, stop=True)
                pe.matmul(misc[:, 80:88], ones[:, :], mk[:, 0, :], start=True, stop=False)
                pe.matmul(misc[:, 80:88], ones[:, :], mk[:, 1, :], start=False, stop=True).then_inc(ranked, 1)
                pe.wait_ge(counts_ok, 1)
                pe.wait_ge(tok_ok, 4)
                with pe.Fori(0, EXPERTS) as e:
                    n = pe.value_load(counts[0:1, bass.ds(e, 1)], min_val=0, max_val=T)
                    with pe.If(n <= P):
                        expert(1, e)
                    with pe.Else():
                        expert(2, e)

            pe.wait_ge(consts, 2)
            norm(0)
            pe.wait_ge(band_in, 16)
            for i in range(8):
                if i >= 4:
                    pe.wait_ge(bias_ok, i - 3)
                pe.matmul(quad[i % 4], flip[:, :], band[:, 2 * i:2 * i + 2, :], start=True, stop=True).then_inc(flipped, 1)
            pe.wait_ge(ident_ok, 1)
            for l in range(DEPTH):
                if l:
                    norm(3 * l)
                mixer(l)
                norm(3 * l + 1)
                dense(l) if l % 2 == 0 else moe(l)
                norm(3 * l + 2)
                ple(l)

        @block.vector
        def _(dve):
            step = Steps(dve, dve_step)

            def bias_lines():
                step(dve.memset(u_line, MASKED))
                step(dve.memset(u_zero, 0.0))
                dve.wait_ge(rel_in, 16)
                step.settle()
                for b in range(BUCKETS):
                    ds_ = [d for d in range(WINDOW) if bucket_of(d) == b]
                    if not ds_:
                        continue
                    j0, j1 = BAND - 1 - ds_[-1], BAND - ds_[0]
                    step(dve.tensor_scalar(u_line[:, j0:j1], u_zero[:, 0:j1 - j0], rel[:, b:b + 1], None, ALU.add))
                step.settle()
                dve.sem_inc(line_ok, 1)

            def decays():
                lam = col[:, C_LAM:C_LAM + DEPTH, :]
                y, z, q = decay[:, 1, :, :], decay[:, 2, :, :], decay[:, 0, :, :]
                t2 = small[:, 66:82].rearrange("p (l k) -> p l k", l=DEPTH)
                dve.wait_ge(small_in, 48)
                step(dve.tensor_scalar(z, lam, -1.0, None, ALU.mult))
                step.settle()
                dve.tensor_tensor(decay[:, 0, :, :], lam, z, ALU.max).then_inc(abs_lam, 1)
                dve.wait_ge(exp_lam, 1)
                step(dve.tensor_scalar(z, y, 2.0, None, ALU.add))
                step.settle()
                step(dve.reciprocal(t2, z))
                step.settle()
                step(dve.tensor_tensor(z, y, t2, ALU.mult))
                step.settle()
                step(dve.tensor_tensor(t2, z, z, ALU.mult))
                step.settle()
                step(dve.tensor_scalar(q, t2, 1.0 / 21, None, ALU.mult))
                for n in range(9, 0, -1):
                    step.settle()
                    step(dve.scalar_tensor_tensor(out=q, in0=q, scalar=1.0 / (2 * n + 1), in1=t2, op0=ALU.add, op1=ALU.mult))
                step.settle()
                step(dve.scalar_tensor_tensor(out=q, in0=q, scalar=1.0, in1=z, op0=ALU.add, op1=ALU.mult))
                step(dve.tensor_scalar(t2, lam, -1.0, 0.0, ALU.mult, ALU.max))
                step.settle()
                step(dve.scalar_tensor_tensor(out=t2, in0=q, scalar=2.0, in1=t2, op0=ALU.mult, op1=ALU.add))
                step.settle()
                step(dve.tensor_scalar(decay[:, 1, :, :], t2, -LRU_C, None, ALU.mult))
                step(dve.tensor_scalar(decay[:, 2, :, :], t2, LRU_C / 2, None, ALU.mult))
                step(dve.tensor_scalar(row[:, R_Q:R_Q + DEPTH * HD], row[:, R_Q:R_Q + DEPTH * HD], HD ** -0.5, None, ALU.mult))
                step.settle()

            def norm(n):
                gain = col[:, (C_MIX, C_FFN, C_PLE)[n % 3] + n // 3, :]
                dve.wait_ge(rooted, n + 1)
                step(dve.reciprocal(rinv, rms))
                step.settle()
                if n == 0:
                    dve.wait_ge(small_in, 48)
                for k in range(KT):
                    dve.scalar_tensor_tensor(out=xnT[:, k, :], in0=hT[:, k, :], scalar=gain[:, k:k + 1], in1=rinv,
                                             op0=ALU.mult, op1=ALU.mult).then_inc(normed, 1)

            def qk_norm(l):
                for i in range(6):
                    c, tt = i // 2, i % 2
                    n = 512 if c < 2 else 256
                    h = n // HD
                    b = 8 * (i % 2)
                    dve.wait_ge(qk_squared, 6 * l + i + 1)
                    dve.tensor_reduce(small[:, b:b + h], sqs[:, i % 2, 0:n].rearrange("p (h d) -> p h d", h=h),
                                      AX_X, ALU.add).then_inc(qk_summed, 1)
                    dve.wait_ge(qk_rooted, 6 * l + i + 1)
                    step(dve.reciprocal(small[:, b + 48:b + 48 + h], small[:, b + 16:b + 16 + h]))
                    step.settle()
                    ps = bank_of(l, "qkv", c, tt)[:, 0:n].rearrange("p (h d) -> p h d", h=h)
                    rb = small[:, b + 48:b + 48 + h].unsqueeze(2).to_broadcast([P, h, HD])
                    if c < 2:
                        q = q_tok[:, tt, 512 * c:512 * c + 512].rearrange("p (h d) -> p h d", h=h)
                        gb = row[:, R_Q + HD * l:R_Q + HD * l + HD].unsqueeze(1).to_broadcast([P, h, HD])
                        taken(dve.tensor_tensor(q, ps, rb, ALU.mult), l, "qkv", c, tt)
                        bk, m = place[(l, "qkv", c, tt)]
                        dve.wait_ge(work_free[bk], m + 1)
                        dve.tensor_tensor(q, q, gb, ALU.mult).then_inc(qk_normed, 1)
                    else:
                        kd = k_dup[:, tt, :, :, :]
                        gb = row[:, R_K + HD * l:R_K + HD * l + HD].unsqueeze(1).to_broadcast([P, h, HD])
                        taken(dve.tensor_tensor(kd[:, :, 0, :], ps, rb, ALU.mult), l, "qkv", c, tt)
                        bk, m = place[(l, "qkv", c, tt)]
                        dve.wait_ge(work_free[bk], m + 1)
                        step(dve.tensor_tensor(kd[:, :, 0, :], kd[:, :, 0, :], gb, ALU.mult))
                        step.settle()
                        dve.tensor_copy(kd[:, :, 1, :], kd[:, :, 0, :]).then_inc(qk_normed, 1)

            def add_bias(l, u):
                g = UNITS * l + u
                b, t = divmod(u, PAIRS)
                w = P * (b + 1)
                m = 32 + 8 * (u % 2)
                dve.wait_ge(scored, g + 1)
                if u >= 2:
                    dve.wait_ge(probs_turned, g - 1)
                e = ebuf[:, u % 2, :, 0:w]
                dve.tensor_tensor(e, score_ps[:, :, 0:w], bias[:, 2 * t:2 * t + 2, BAND - w:BAND], ALU.add).then_inc(biased, 1)
                dve.wait_ge(biased, g + 1)
                sink = row[:, R_SINK + HEADS * l + 2 * t:R_SINK + HEADS * l + 2 * t + 2]
                step(dve.tensor_reduce(small[:, m:m + 2], e, AX_X, ALU.max))
                step.settle()
                step(dve.tensor_tensor(small[:, m:m + 2], small[:, m:m + 2], sink, ALU.max))
                step.settle()
                dve.tensor_scalar(small[:, m + 2:m + 4], small[:, m:m + 2], -1.0, None, ALU.mult)
                dve.tensor_tensor(small[:, m + 4:m + 6], sink, small[:, m:m + 2], ALU.subtract).then_inc(max_ok, 1)

            def probs(l, u):
                g = UNITS * l + u
                w = P * (u // PAIRS + 1)
                m = 32 + 8 * (u % 2)
                dve.wait_ge(exped, g + 1)
                step(dve.tensor_tensor(small[:, m:m + 2], small[:, m + 4:m + 6], small[:, m + 6:m + 8], ALU.add))
                step.settle()
                step(dve.reciprocal(small[:, m:m + 2], small[:, m:m + 2]))
                step.settle()
                for hh in range(2):
                    e = ebuf[:, u % 2, hh, 0:w]
                    ins = dve.tensor_scalar(e, e, small[:, m + hh:m + hh + 1], None, ALU.mult)
                ins.then_inc(probs_ok, 1)

            def conv(l, c):
                bk, n = place[(l, "lx", c)]
                dve.wait_ge(work_free[bk], n + 1)
                x = lru[:, c, :]
                o = xcT[:, c, :]
                w = [col[:, C_CONV + CONV * l + j, c:c + 1] for j in range(CONV)]
                step(dve.tensor_scalar(o, x[:, 0:T], w[0], col[:, C_CB + l, c:c + 1], ALU.mult, ALU.add))
                for j in range(1, CONV):
                    step.settle()
                    ins = dve.scalar_tensor_tensor(out=o, in0=x[:, j:j + T], scalar=w[j], in1=o, op0=ALU.mult, op1=ALU.add)
                    if j < CONV - 1:
                        step(ins)
                ins.then_inc(conv_done, 1)

            def recurrence(l):
                for c in range(KT):
                    dve.wait_ge(sqrt_ok, KT * l + c + 1)
                    step(dve.scalar_tensor_tensor(out=rT[:, c, :], in0=decayT[:, c, :], scalar=1.0, in1=rT[:, c, :],
                                                  op0=ALU.add, op1=ALU.mult))
                    step.settle()
                    step(dve.tensor_tensor(rT[:, c, :], rT[:, c, :], lru[:, c, CONV - 1:], ALU.mult))
                    step.settle()
                    step(dve.tensor_tensor_scan(xcT[:, c, :], decayT[:, c, :], rT[:, c, :], 0.0, ALU.mult, ALU.add))

            def mixer(l):
                qk_norm(l)
                for g in range(3 * KT):
                    s = g - FIRST_UNIT
                    if 0 <= s < UNITS:
                        add_bias(l, s)
                    if 0 <= g - FIRST_UNIT - 2 < KT:
                        conv(l, g - FIRST_UNIT - 2)
                    if 0 <= s - 1 < UNITS:
                        probs(l, s - 1)
                for j in range(KT):
                    wait_full(dve, l, "pa", j)
                    if j == 0:
                        dve.wait_ge(sig_ga, l + 1)
                    taken(dve.tensor_tensor(gate_a[:, j, :], gate_a[:, j, :], bank_of(l, "pa", j)[:, 0:T], ALU.mult), l, "pa", j)
                    dve.wait_ge(sig_ri, KT * l + j + 1)
                    step(dve.tensor_tensor(lru[:, j, CONV - 1:], lru[:, j, CONV - 1:], xcT[:, j, :], ALU.mult))
                recurrence(l)
                step.settle()
                for j in range(KT):
                    bk, n = place[(l, "lg", j)]
                    dve.wait_ge(work_free[bk], n + 1)
                    dve.tensor_tensor(xcT[:, j, :], xcT[:, j, :], glgT[:, j, :], ALU.mult).then_inc(yb_ok, 1)
                dve.wait_ge(sig_gb, l + 1)
                for j in range(KT):
                    wait_full(dve, l, "pb", j)
                    taken(dve.tensor_tensor(gate_b[:, j, :], gate_b[:, j, :], bank_of(l, "pb", j)[:, 0:T], ALU.mult), l, "pb", j)
                    bk, n = place[(l, "pb", j)]
                    dve.wait_ge(work_free[bk], n + 1)
                    dve.tensor_tensor(gate_a[:, j, :], gate_a[:, j, :], gate_b[:, j, :], ALU.add).then_inc(merged, 1)
                for j in range(KT):
                    wait_full(dve, l, "out", j)
                    ins = dve.tensor_tensor(hT[:, j, :], hT[:, j, :], bank_of(l, "out", j)[:, 0:T], ALU.add)
                    ins.then_inc(h_mixed, 1)
                    dve.wait_ge(h_mixed, KT * l + j + 1)
                    dve.sem_inc(work_free[place[(l, "out", j)][0]], 1)

            def dense(l):
                for i in range(FC * FT):
                    c, ft = divmod(i, FT)
                    wait_full(dve, l, "ffn", c, ft)
                    dve.wait_ge(silu_ok, FC * FT * (l // 2) + i + 1)
                    dve.tensor_tensor(hid[:, c % 2, ft, :], silu_buf[:, i % 2, :], bank_of(l, "ffn", c, ft)[:, T:2 * T],
                                      ALU.mult).then_inc(hid_ok, 1)
                    dve.wait_ge(hid_ok, FC * FT * (l // 2) + i + 1)
                    dve.sem_inc(work_free[place[(l, "ffn", c, ft)][0]], 1)
                dve.wait_ge(ffn_acc, FC * (l // 2 + 1))
                for b in range(4):
                    dve.tensor_tensor(hT[:, 2 * b:2 * b + 2, :], hT[:, 2 * b:2 * b + 2, :],
                                      quad[b].rearrange("p (k t) -> p k t", k=2), ALU.add).then_inc(h_ffn, 1)

            def ple(l):
                for j in range(KT):
                    wait_full(dve, l, "ple", j)
                    dve.wait_ge(ple_gate, KT * l + j + 1)
                    s = silu_buf[:, j % 2, :]
                    taken(dve.tensor_tensor(s, s, bank_of(l, "ple", j)[:, T:2 * T], ALU.mult), l, "ple", j)
                    bk, n = place[(l, "ple", j)]
                    dve.wait_ge(work_free[bk], n + 1)
                    dve.tensor_tensor(hT[:, j, :], hT[:, j, :], s, ALU.add).then_inc(h_ple, 1)

            def routing():
                L, EQ, V, MK1, MK2, GT, MK = (route[:, n, :, :] for n in (0, 1, 2, 3, 4, 5, M_MASK))
                m1, m2, df, ex, w1, w2 = (rsmall[:, n, :] for n in range(6))
                mv = rsmall[:, 6, :]

                def wide(a):
                    return a.unsqueeze(2).to_broadcast([P, TT, EXPERTS])

                pw = pick_w.unsqueeze(1).to_broadcast([P, TT, EXPERTS])
                rb = row[:, R_RB:R_RB + EXPERTS].unsqueeze(1).to_broadcast([P, TT, EXPERTS])
                dve.wait_ge(logits_done, 1)
                dve.wait_ge(pool_route, 3)
                step(dve.tensor_tensor(L, misc[:, 0:16].rearrange("p (t e) -> p t e", t=TT), rb, ALU.add))
                step.settle()
                for m, mk in ((m1, MK1), (m2, MK2)):
                    step(dve.tensor_reduce(m, L, AX_X, ALU.max))
                    step.settle()
                    step(dve.tensor_tensor(EQ, L, wide(m), ALU.is_equal))
                    step.settle()
                    step(dve.tensor_tensor(V, EQ, pw, ALU.mult))
                    step.settle()
                    step(dve.tensor_reduce(mv, V, AX_X, ALU.max))
                    step.settle()
                    step(dve.tensor_tensor(mk, V, wide(mv), ALU.is_equal))
                    step.settle()
                    if mk is MK1:
                        step(dve.scalar_tensor_tensor(out=L, in0=mk, scalar=-3e38, in1=L, op0=ALU.mult, op1=ALU.add))
                        step.settle()
                step(dve.tensor_tensor(MK, MK1, MK2, ALU.add))
                step.settle()
                dve.sem_inc(route_masks, 1)
                dve.tensor_tensor(df, m2, m1, ALU.subtract).then_inc(route_diff, 1)
                dve.wait_ge(route_exp, 1)
                step(dve.tensor_scalar(w2, ex, 1.0, None, ALU.add))
                step.settle()
                step(dve.reciprocal(w1, w2))
                step.settle()
                step(dve.tensor_tensor(w2, ex, w1, ALU.mult))
                step(dve.tensor_tensor(MK1, MK1, wide(w1), ALU.mult))
                step.settle()
                step(dve.tensor_tensor(MK2, MK2, wide(w2), ALU.mult))
                step(dve.memset(gate_m, 0.0))
                step(dve.memset(rank_m, -1.0))
                step.settle()
                step(dve.tensor_tensor(gate_m[:, :, 0:EXPERTS], MK1, MK2, ALU.add))
                dve.wait_ge(ranked, 1)
                step(dve.tensor_scalar(GT, misc[:, 64:80].rearrange("p (t e) -> p t e", t=TT), 1.0, None, ALU.add))
                step.settle()
                step(dve.tensor_tensor(GT, GT, MK, ALU.mult))
                step.settle()
                step(dve.tensor_scalar(rank_m[:, :, 0:EXPERTS], GT, -1.0, None, ALU.add))
                step(dve.tensor_copy(counts, misc[:, 80:88]))
                step.settle()
                dve.sem_inc(counts_ok, 1)

            def build(e):
                for tt in range(TT):
                    dve.tensor_scalar(m_pick[:, tt, :], iota_f, rank_m[:, tt, bass.ds(e, 1)], None, ALU.is_equal)
                    ins = dve.tensor_scalar(m_gpick[:, tt, :], iota_f, rank_m[:, tt, bass.ds(e, 1)],
                                            gate_m[:, tt, bass.ds(e, 1)], ALU.is_equal, ALU.mult)
                ins.then_inc(m_built, 1)

            def expert(tiles, e):
                w = 2 // tiles
                for st in range(tiles):
                    dve.wait_ge(m_full[1], e * 16 + w * (st + 1))
                    dve.tensor_copy(xg[:, st, 4:8, :], work[1][:, :].rearrange("p (k n) -> p k n", k=4)).then_inc(m_taken[1], w)
                for c in range(FC):
                    for st in range(tiles):
                        it = c * tiles + st
                        dve.wait_ge(m_taken[0], e * 16 + (1 + w * (tiles + it + 1)))
                        dve.wait_ge(m_full[1], e * 16 + w * (tiles + it + 1))
                        dve.tensor_tensor(m_hid[st], m_silu, work[1][:, :], ALU.mult).then_inc(m_taken[1], w)
                    if c == 2:
                        dve.wait_ge(m_gturned, e * 2 + 2)
                        build(e + 1)
                for st in range(tiles):
                    for q in range(4):
                        i = 4 * st + q
                        dve.wait_ge(m_combined, e * 8 + w * (i + 1))
                        if st:
                            dve.wait_ge(m_added, e * 8 + (1 + w * (i - 3)))
                        elif q == 0:
                            dve.wait_ge(m_added, e * 8 + 1)
                        dve.tensor_tensor(hT[:, 2 * q:2 * q + 2, :], hT[:, 2 * q:2 * q + 2, :],
                                          (pv_ps, misc)[q % 2][:, :].rearrange("p (k t) -> p k t", k=2),
                                          ALU.add).then_inc(m_added, w)

            def moe(l):
                routing()
                dve.sem_inc(m_taken[1], 1)
                dve.sem_inc(m_added, 1)
                build(0)
                with dve.Fori(0, EXPERTS) as e:
                    n = dve.value_load(counts[0:1, bass.ds(e, 1)], min_val=0, max_val=T)
                    with dve.If(n <= P):
                        expert(1, e)
                    with dve.Else():
                        expert(2, e)

            step(dve.memset(small[:, 64:65], EPS))
            step(dve.memset(lru[:, :, 0:CONV - 1], 0.0))
            bias_lines()
            decays()
            norm(0)
            for l in range(DEPTH):
                if l:
                    norm(3 * l)
                mixer(l)
                norm(3 * l + 1)
                dense(l) if l % 2 == 0 else moe(l)
                norm(3 * l + 2)
                ple(l)


def feature_cols(a):
    return a.reshape(-1, KT, P).transpose(2, 0, 1)


def column_chunks(w):
    n = w.shape[1] // CW
    return w.reshape(KT, P, n, CW).transpose(2, 1, 0, 3).reshape(n, P, CHUNK)


def row_chunks(w):
    return w.reshape(FC, FT, P, D).transpose(0, 2, 1, 3).reshape(FC, P, CHUNK)


def ffn_blocks(w1, w3, w2):
    parts = {"w1": column_chunks(w1), "w3": column_chunks(w3), "w2": row_chunks(w2)}
    return [parts[w][c] for w, c in ffn_order()]


def kernel(**inputs):
    import concourse.bacc as _bacc
    from concourse.bass_utils import run_bass_kernel_spmd as _run

    a = {k: np.asarray(v) for k, v in inputs.items()}
    asc = np.ascontiguousarray
    mix = []
    for l in range(DEPTH):
        win = column_chunks(a["w_in"][l])
        mix += [win[c] for c in W_IN_ORDER]
        mix += list(column_chunks(a["w_proj_attn"][l]))
        mix += [win[c] for c in W_IN_LG]
        mix += list(column_chunks(a["w_proj_lru"][l])) + list(column_chunks(a["w_out"][l]))
    moe = []
    for e in range(EXPERTS):
        moe += ffn_blocks(a["moe_w1"][0, e], a["moe_w3"][0, e], a["moe_w2"][0, e])
    cols = np.concatenate([
        a["mix_norm"], a["ffn_norm"], a["ple_norm"], a["conv_w"].reshape(DEPTH * CONV, D), a["conv_b"],
        a["b_rg"].reshape(DEPTH, D), a["b_ig"].reshape(DEPTH, D), a["lru_lambda"]])
    rows = np.concatenate([a["q_norm"].reshape(-1), a["k_norm"].reshape(-1), a["sinks"].reshape(-1),
                           a["router_b"].reshape(-1)])
    arrays = {
        "xT": a["x"][0].T.reshape(KT, P, T).transpose(1, 0, 2),
        "pT": a["p"][:, 0].transpose(0, 2, 1).reshape(DEPTH, PLE // P, P, T).transpose(2, 0, 1, 3),
        "cols": feature_cols(cols),
        "rows": np.broadcast_to(rows[None, :], (P, rows.shape[0])),
        "relT": a["rel_bias"].T,
        "w_rg": a["w_rg"].reshape(DEPTH, KT, 2, HD, HD).transpose(0, 2, 3, 1, 4).reshape(DEPTH, P, KT, HD),
        "w_ig": a["w_ig"].reshape(DEPTH, KT, 2, HD, HD).transpose(0, 2, 3, 1, 4).reshape(DEPTH, P, KT, HD),
        "router": a["router_w"][0].reshape(KT, P, EXPERTS).transpose(1, 0, 2),
        "mix_w": np.stack(mix).reshape(DEPTH, MIX_CHUNKS, P, CHUNK),
        "dense_w": np.stack(ffn_blocks(a["dense_w1"][0], a["dense_w3"][0], a["dense_w2"][0])),
        "moe_w": np.stack(moe).reshape(EXPERTS, FFN_CHUNKS, P, CHUNK),
        "ple_w": np.stack([column_chunks(a["ple_gate_w"][l]) for l in range(DEPTH)]),
        "ple_p": a["ple_proj_w"].reshape(DEPTH, PLE // P, P, D).transpose(0, 2, 1, 3).reshape(DEPTH, P, 2 * D),
    }
    nc = _bacc.Bacc("TRN2", target_bir_lowering=False, num_devices=1)
    arrays = {f"in_{k}": asc(v) for k, v in arrays.items()}
    args = [nc.dram_tensor(k, v.shape, mybir.dt.from_np(v.dtype), kind="ExternalInput").ap() for k, v in arrays.items()]
    bias_line = nc.dram_tensor("bias_line", (HEADS, U_LEN), F32)
    out = nc.dram_tensor("out_T", (P, KT, T), F32, kind="ExternalOutput").ap()
    trunk(nc, *args, bias_line, out)
    r = _run(nc, [arrays], core_ids=[0])
    got = r.results[0]["out_T"]
    return np.ascontiguousarray(got.transpose(2, 1, 0).reshape(1, T, D))
```

```python
import math
from contextlib import ExitStack

import numpy as np

import concourse.bass as bass
from concourse import mybir

F32 = mybir.dt.float32
F32R = mybir.dt.float32r
I32 = mybir.dt.int32
ALU = mybir.AluOpType
ACT = mybir.ActivationFunctionType
AX_X = mybir.AxisListType.X

P = 128
D = 1024
T = 256
DEPTH = 2
KT = D // P
TT = T // P
HEADS = 16
KV_HEADS = 4
HD = 64
PAIRS = HEADS // 2
BAND = 256
WINDOW = 128
BUCKETS = 32
MAX_EXACT = BUCKETS // 2
MAX_DISTANCE = 128
CONV = 4
LRU_C = 8.0
LRU_BLOCKS = 16
D_FF = D * 7 // 2
EXPERTS = 8
PLE = 256
EPS = 1e-6
MASKED = -1e30
CW = 512
CHUNK = KT * CW
FT = CW // P
FC = D_FF // CW
RING = 3
QUARTER = CHUNK // 4
UNITS_HELD = 6
AHEAD = 4
MIX_CHUNKS = 17
FFN_CHUNKS = 3 * FC
PLE_CHUNKS = 2
EXTRA = (2 * T) // (P + 1)
JOBS = EXPERTS + EXTRA
JOB_Q = 4 * FFN_CHUNKS
U_LEN = 384

W_IN_ORDER = [0, 1, 2, 3, 4, 9, 10, 7, 8]
W_IN_LG = [5, 6]


def bucket_of(dist):
    if dist < MAX_EXACT:
        return dist
    f = np.float32(np.log(np.float32(dist) / np.float32(MAX_EXACT)))
    f = np.float32(f / np.float32(math.log(MAX_DISTANCE / MAX_EXACT))) * np.float32(BUCKETS - MAX_EXACT)
    return min(MAX_EXACT + int(f), BUCKETS - 1)


def ffn_order():
    order = []
    for c in range(FC):
        order += [("w1", c), ("w3", c)]
        if c:
            order.append(("w2", c - 1))
    return order + [("w2", FC - 1)]


def mixer_groups():
    groups = [("qkv", c, tt) for c in range(3) for tt in range(TT)]
    for name in ("lx", "gb", "ga", "pa", "lg", "pb", "out"):
        groups += [(name, j) for j in range(KT)]
    return groups


class Steps:

    def __init__(self, eng, sem):
        self.eng, self.sem, self.n = eng, sem, 0

    def __call__(self, ins):
        self.n += 1
        ins.then_inc(self.sem, 1)

    def settle(self):
        self.eng.wait_ge(self.sem, self.n)


def trunk(nc, xT, pT, cols, rows, relT, wrg_d, wig_d, router_d, mix_w, dense_w, moe_w, ple_w, ple_p, bias_line, outT):
    groups = []
    for l in range(DEPTH):
        groups += [(l, *g) for g in mixer_groups()]
        if l % 2 == 0:
            groups += [(l, "ffn", c, ft) for c in range(FC) for ft in range(FT)]
        groups += [(l, "ple", j) for j in range(KT)]
    own = {g: (2 + TT * (g[2] - 1) + g[3], g[0]) for g in groups if g[1] == "qkv" and g[2]}
    place = {g: (i % 2, i // 2) for i, g in enumerate(g for g in groups if g not in own)}
    place.update(own)

    at = {}
    n_chunks = 0
    moe_chunk = None
    for l in range(DEPTH):
        for i in range(MIX_CHUNKS):
            at[(l, "mix", i)] = n_chunks
            n_chunks += 1
        if l % 2 == 0:
            for w, c in ffn_order():
                at[(l, w, c)] = n_chunks
                n_chunks += 1
        else:
            moe_chunk = n_chunks
            n_chunks += JOBS * FFN_CHUNKS
        for i in range(PLE_CHUNKS):
            at[(l, "ple", i)] = n_chunks
            n_chunks += 1
    FFN_AT = {wc: i for i, wc in enumerate(ffn_order())}
    MIX_AT = {"qkv": 0, "lx": 3, "gb": 5, "ga": 7, "pa": 9, "lg": 11, "pb": 13, "out": 15}

    quarters = []
    phase_q = {}
    for l in range(DEPTH):
        phase_q[(l, "mix")] = len(quarters)
        for c in range(3):
            quarters += [(l, "rows", (l, "mix", c), q, ("qkv", c, q)) for q in range(4)]
        for name in ("lx", "gb", "ga", "pa", "lg", "pb", "out"):
            quarters += [(l, "cols", (l, "mix", MIX_AT[name] + j // FT), j % FT, (name, j)) for j in range(KT)]
        phase_q[(l, "ffn")] = len(quarters)
        if l % 2 == 0:
            for c in range(FC + 1):
                if c < FC:
                    for ft in range(FT):
                        quarters += [(l, "cols", (l, "w1", c), ft, ("ffn", c, ft)), (l, "cols", (l, "w3", c), ft, ("ffn", c, ft))]
                if c:
                    quarters += [(l, "rows", (l, "w2", c - 1), ft, ("w2", c - 1, ft)) for ft in range(FT)]
        else:
            quarters += [None] * (JOBS * JOB_Q)
        phase_q[(l, "ple")] = len(quarters)
        quarters += [(l, "cols", (l, "ple", j // FT), j % FT, ("ple", j)) for j in range(KT)]
    q_at = {(q[2], q[3]): i for i, q in enumerate(quarters) if q}
    chunk_split = {}
    for i, q in enumerate(quarters):
        if q:
            chunk_split[at[q[2]]] = i + 1
    for n in range(JOBS * FFN_CHUNKS):
        chunk_split[moe_chunk + n] = 4 * (moe_chunk + n + 1)
    assert len(quarters) == 4 * n_chunks

    with ExitStack() as ctx:
        def sb(name, shape, dt=F32):
            return ctx.enter_context(nc.sbuf_tensor(name, shape, dt))

        def sem(name):
            return ctx.enter_context(nc.semaphore(name))

        def shared(name, n):
            with nc.sbuf_tensor(name, [P, n], F32) as plain:
                pass
            return plain, sb(name + "_r", [P, n], F32R)

        raw = [sb(f"raw{i}", [P, CHUNK]) for i in range(RING)]
        w_hi = [sb(f"w_hi{i}", [P, QUARTER], F32R) for i in range(UNITS_HELD)]
        w_lo = [sb(f"w_lo{i}", [P, QUARTER], F32R) for i in range(UNITS_HELD)]
        hT = sb("hT", [P, KT, T])
        x1, x1_r = shared("x1", KT * T)
        x2, x2_r = shared("x2", KT * T)
        areaA, areaA_r = shared("areaA", KT * T)
        areaB, areaB_r = shared("areaB", KT * T)
        areaK = sb("areaK", [P, KT * T])
        gate_a_flat, gate_a_r = shared("gate_a", KT * T)
        gate_b_flat = sb("gate_b", [P, KT * T])
        spare, spare_r = shared("spare", CHUNK)
        bias_flat, bias_r = shared("bias", HEADS * BAND)
        lru = sb("lru", [P, KT, CONV - 1 + T])
        v_sb = sb("v_sb", [P, TT, KV_HEADS * HD])
        ident = sb("ident", [P, P])
        ones = sb("ones", [P, P])
        flip = sb("flip", [P, P])
        NCOL = cols.shape[1]
        col = sb("col", [P, NCOL, KT])
        NROW = rows.shape[1]
        row = sb("row", [P, NROW])
        rel = sb("rel", [HEADS, BUCKETS])
        decay = sb("decay", [P, 3, DEPTH, KT])
        small = sb("small", [P, 96])

        def by_feature(area):
            return area[:, 0:KT * T].rearrange("p (k t) -> p k t", k=KT)

        bias = bias_flat[:, :].rearrange("p (h s) -> p h s", h=HEADS)
        gate_a, gate_b = by_feature(gate_a_flat), by_feature(gate_b_flat)
        merged_lo = by_feature(gate_a_r)
        squares, xn_hi = by_feature(x1), by_feature(x1_r)
        xnT, xn_lo = by_feature(x2), by_feature(x2_r)

        q_tok = areaA[:, :].rearrange("p (t n) -> p t n", t=TT)
        yaT = by_feature(areaA)
        glgT = yaT
        qT = by_feature(areaB)
        ya_hi, ya_lo = by_feature(areaB_r), by_feature(areaA_r)
        yb_hi, yb_lo = by_feature(areaB_r), by_feature(spare_r)
        merged_hi = by_feature(areaA_r)
        decayT = by_feature(areaK)
        k_dup = areaK[:, 0:1024].rearrange("p (t g s d) -> p t g s d", t=TT, g=KV_HEADS, s=2)
        k_dup2 = areaK[:, 0:1024].rearrange("p (t g n) -> p t g n", t=TT, g=KV_HEADS)
        kTT = areaK[:, 1024:2048].rearrange("p (g t) -> p g t", g=KV_HEADS)
        wrg = areaK[:, 0:512].rearrange("p (k d) -> p k d", k=KT)
        wig = areaK[:, 512:1024].rearrange("p (k d) -> p k d", k=KT)
        wpp = areaK[:, :].rearrange("p (k n) -> p k n", k=PLE // P)
        p_sb = v_sb
        silu_buf = gate_b_flat[:, 0:512].rearrange("p (b t) -> p b t", b=2)
        rms = gate_b_flat[:, 512:768]
        rinv = gate_b_flat[:, 768:1024]
        xcT = by_feature(spare)
        rT = spare[:, 2048:4096].rearrange("p (k t) -> p k t", k=KT)
        ebuf = spare[:, 2048:3072].rearrange("p (b h s) -> p b h s", b=2, h=2)
        ptb = spare[:, 3072:4096].rearrange("p (b h s) -> p b h s", b=2, h=2)
        sqs = spare[:, 2048:3072].rearrange("p (b n) -> p b n", b=2)
        bands = [area[:, :].rearrange("p (h s) -> p h s", h=HEADS // 2) for area in (gate_a_flat, areaB)]
        u_line = gate_a_flat[0:HEADS, 0:U_LEN]
        u_zero = gate_a_flat[0:HEADS, U_LEN:U_LEN + P]

        work_ps = [ctx.enter_context(nc.psum_tensor(f"work{i}", [P, 512], F32)) for i in range(2)]
        acc = [ctx.enter_context(nc.psum_tensor(f"acc{i}", [P, 1024], F32)) for i in range(2)]
        pv_ps = ctx.enter_context(nc.psum_tensor("pv_ps", [P, 512], F32))
        misc = ctx.enter_context(nc.psum_tensor("misc", [P, 512], F32))
        quad = [acc[0][:, 0:512], acc[0][:, 512:1024], acc[1][:, 0:512], acc[1][:, 512:1024]]
        work = [work_ps[0][:, :], work_ps[1][:, :]] + quad

        score_ps = acc[0][:, :].rearrange("p (h s) -> p h s", h=2)

        slot_full = [sem(f"slot_full{i}") for i in range(RING)]
        work_full = [sem(f"work_full{i}") for i in range(6)]
        work_free = [sem(f"work_free{i}") for i in range(6)]
        x_in = sem("x_in")
        small_in = sem("small_in")
        rows_in = sem("rows_in")
        rel_in = sem("rel_in")
        gates_in = sem("gates_in")
        line_out = sem("line_out")
        band_in = sem("band_in")
        consts = sem("consts")
        ident_ok = sem("ident_ok")
        line_ok = sem("line_ok")
        eps_ok = sem("eps_ok")
        flipped = sem("flipped")
        bias_ok = sem("bias_ok")
        exp_lam = sem("exp_lam")
        abs_lam = sem("abs_lam")
        dve_step = sem("dve_step")
        pool_step = sem("pool_step")
        squared = sem("squared")
        summed = sem("summed")
        rooted = sem("rooted")
        normed = sem("normed")
        h_mixed = sem("h_mixed")
        h_ffn = sem("h_ffn")
        h_ple = sem("h_ple")
        qk_squared = sem("qk_squared")
        qk_summed = sem("qk_summed")
        qk_rooted = sem("qk_rooted")
        qk_normed = sem("qk_normed")
        qk_turned = sem("qk_turned")
        qkT_ok = sem("qkT_ok")
        scored = sem("scored")
        biased = sem("biased")
        max_ok = sem("max_ok")
        exped = sem("exped")
        probs_ok = sem("probs_ok")
        probs_turned = sem("probs_turned")
        probsT_ok = sem("probsT_ok")
        pv_done = sem("pv_done")
        pv_taken = sem("pv_taken")
        conv_done = sem("conv_done")
        ri_done = sem("ri_done")
        sig_ga = sem("sig_ga")
        sig_ri = sem("sig_ri")
        sig_gb = sem("sig_gb")
        decay_ok = sem("decay_ok")
        tanh_ok = sem("tanh_ok")
        sqrt_ok = sem("sqrt_ok")
        yb_ok = sem("yb_ok")
        merged = sem("merged")
        silu_ok = sem("silu_ok")
        hid_ok = sem("hid_ok")
        hid_read = sem("hid_read")
        ffn_acc = sem("ffn_acc")
        ple_gate = sem("ple_gate")
        out_done = sem("out_done")

        xn_tok = q_tok
        xg_hi = bias_r[:, 0:1024].rearrange("p (k n) -> p k n", k=KT)
        xg_lo = bias_r[:, 1024:2048].rearrange("p (k n) -> p k n", k=KT)
        hidT_hi = bias_r[:, 2048:2560].rearrange("p (f n) -> p f n", f=FT)
        hidT_lo = bias_r[:, 2560:3072].rearrange("p (f n) -> p f n", f=FT)
        y_sb = spare[:, 0:D]
        scr = lru[:, :, :].rearrange("p k t -> p (k t)")
        m_silu = scr[:, 0:512]
        m_hid = scr[:, 512:1024]
        gbf = gate_b_flat
        m_pick = gbf[:, 0:256].rearrange("p (t n) -> p t n", t=TT)
        m_gpick = gbf[:, 256:512].rearrange("p (t n) -> p t n", t=TT)
        m_gpickT = gbf[:, 1024:1280]
        iota_f = gbf[:, 1536:1664]
        gaf = gate_a_flat
        before = gaf[:, 0:P]
        iota_i = gaf[:, 512:640].bitcast(I32)
        route = gaf[:, 1024:1280].rearrange("p (n t e) -> p n t e", n=16, t=TT)
        rank_m = gaf[:, 1536:1568].rearrange("p (t e) -> p t e", t=TT)
        gate_m = gaf[:, 1568:1600].rearrange("p (t e) -> p t e", t=TT)
        pick_w = gaf[:, 1600:1608]
        pick_wi = gaf[:, 1608:1616].bitcast(I32)
        over = gaf[:, 1664:1728].rearrange("p (n e) -> p n e", e=EXPERTS)
        extra_n = gaf[:, 1728:1731].bitcast(I32)
        extra_id = gaf[:, 1736:1739].bitcast(I32)
        rw = gaf[:, 1792:1856].rearrange("p (k e) -> p k e", k=KT)
        rsmall = gaf[:, 1632:1664].rearrange("p (n t) -> p n t", t=TT)

        logits_done = sem("logits_done")
        tok_turned = sem("tok_turned")
        tok_ok = sem("tok_ok")
        route_masks = sem("route_masks")
        route_diff = sem("route_diff")
        route_exp = sem("route_exp")
        ranked = sem("ranked")
        counts_ok = sem("counts_ok")
        pool_route = sem("pool_route")
        hi_ok = sem("hi_ok")
        split_ok = sem("split_ok")
        rows_used = sem("rows_used")
        ya_split = sem("ya_split")
        ple_in = sem("ple_in")
        router_in = sem("router_in")
        part_used = sem("part_used")
        extra_ok = sem("extra_ok")
        m_built = sem("m_built")
        m_gathered = sem("m_gathered")
        m_xg_hi = sem("m_xg_hi")
        m_xg = sem("m_xg")
        m_silu_ok = sem("m_silu_ok")
        m_hid_ok = sem("m_hid_ok")
        m_turned = sem("m_turned")
        m_hidT_hi = sem("m_hidT_hi")
        m_hidT = sem("m_hidT")
        m_y = sem("m_y")
        m_gturned = sem("m_gturned")
        m_gtaken = sem("m_gtaken")
        m_combined = sem("m_combined")
        m_added = sem("m_added")
        M_MASK = 6
        M_W1 = [4 * FFN_AT[("w1", c)] + 3 for c in range(FC)]
        M_W3 = [4 * FFN_AT[("w3", c)] + 3 for c in range(FC)]
        M_TURN = M_W1[1:] + [4 * FFN_AT[("w2", FC - 1)] - 1]
        M_GT = M_W3[0]
        hid_hi = areaA_r[:, :].rearrange("p (b f t) -> p b f t", b=2, f=FT)
        hid_lo = areaB_r[:, :].rearrange("p (b f t) -> p b f t", b=2, f=FT)

        C_MIX, C_FFN, C_PLE, C_CONV, C_CB, C_RG, C_IG, C_LAM = (
            0, DEPTH, 2 * DEPTH, 3 * DEPTH, 7 * DEPTH, 8 * DEPTH, 9 * DEPTH, 10 * DEPTH)
        R_Q, R_K, R_SINK, R_RB = 0, DEPTH * HD, 2 * DEPTH * HD, 2 * DEPTH * HD + DEPTH * HEADS

        def raw_part(g):
            _, kind, key, q, _ = quarters[g]
            slot = raw[at[key] % RING]
            if kind == "rows":
                return slot[:, q * QUARTER:(q + 1) * QUARTER].rearrange("p (k n) -> p k n", k=KT)
            return slot[:, :].rearrange("p (k n) -> p k n", k=KT)[:, :, q * P:(q + 1) * P]

        def unit(parts, g):
            return parts[g % UNITS_HELD][:, :].rearrange("p (k n) -> p k n", k=KT)

        def wait_read(eng, g):
            l, _, _, _, by = quarters[g]
            if by[0] == "qkv":
                _, c, q = by
                if q < 3:
                    eng.wait_ge(rows_used, 9 * l + 3 * c + q + 1)
                else:
                    wait_full(eng, l, "qkv", c, TT - 1)
            elif by[0] == "w2":
                eng.wait_ge(ffn_acc, FC * FT * (l // 2) + FT * by[1] + by[2] + 1)
            else:
                wait_full(eng, l, *by)

        def split_hi(act, g):
            n = at[quarters[g][2]]
            act.wait_ge(slot_full[n % RING], 16 * (n // RING + 1))
            if g >= UNITS_HELD and quarters[g - UNITS_HELD]:
                wait_read(act, g - UNITS_HELD)
            act.activation(unit(w_hi, g), raw_part(g), ACT.Copy).then_inc(hi_ok, 1)

        def split_lo(eng, g):
            eng.wait_ge(hi_ok, g + 1)
            eng.tensor_tensor(unit(w_lo, g), raw_part(g), unit(w_hi, g).bitcast(F32), ALU.subtract).then_inc(split_ok, 1)

        def bank_of(l, *g):
            b, _ = place[(l, *g)]
            return work[b]

        def taken(ins, l, *g):
            ins.then_inc(work_free[place[(l, *g)][0]], 1)

        def wait_full(eng, l, *g):
            b, n = place[(l, *g)]
            eng.wait_ge(work_full[b], n + 1)

        def wait_h(eng, n, q=3):
            l, part = divmod(n, 3)
            if part == 0 and l == 0:
                eng.wait_ge(x_in, 16)
            elif part == 0:
                eng.wait_ge(h_ple, KT * l)
            elif part == 1:
                eng.wait_ge(h_mixed, KT * l + 2 * q + 2)
            elif l % 2 == 0:
                eng.wait_ge(h_ffn, 4 * (l // 2) + q + 1)
            else:
                eng.wait_ge(m_added, 4 * (JOBS + 1))

        turn_ps = [pv_ps[:, :], misc[:, :], quad[0], quad[1], quad[2], quad[3]]
        FIRST_UNIT = 4
        UNITS = TT * PAIRS

        block = ctx.enter_context(nc.Block())

        @block.sync
        def _(sp):
            def load(key, src):
                n = at[key]
                if n >= RING:
                    sp.wait_ge(split_ok, chunk_split[n - RING])
                sp.dma_start(raw[n % RING][:, :], src).then_inc(slot_full[n % RING], 16)

            def load_expert(e, j, first):
                for i in range(FFN_CHUNKS):
                    n = moe_chunk + first * FFN_CHUNKS + i
                    sp.wait_ge(split_ok, j * JOB_Q + chunk_split[n - RING])
                    sp.dma_start(raw[n % RING][:, :], moe_w[e, i]).then_inc(slot_full[n % RING], 16)

            sp.dma_start(col[:, :, :], cols).then_inc(small_in, 16)
            sp.dma_start(hT[:, :, :], xT).then_inc(x_in, 16)
            for l in range(DEPTH):
                for i in range(MIX_CHUNKS):
                    load((l, "mix", i), mix_w[l, i])
                    if i == 8:
                        sp.wait_ge(qk_turned, 6 * (l + 1))
                        sp.dma_start(wrg, wrg_d[l]).then_inc(gates_in, 16)
                        sp.dma_start(wig, wig_d[l]).then_inc(gates_in, 16)
                    if i == MIX_CHUNKS - 1:
                        sp.wait_ge(pv_done, UNITS * (l + 1))
                        sp.wait_ge(yb_ok, KT * (l + 1))
                        sp.dma_start(p_sb[:, :, :], pT[l]).then_inc(ple_in, 16)
                        sp.dma_start(wpp, ple_p[l].rearrange("p (k n) -> p k n", k=PLE // P)).then_inc(ple_in, 16)
                if l % 2 == 0:
                    for i, (w, c) in enumerate(ffn_order()):
                        load((l, w, c), dense_w[i])
                else:
                    with sp.Fori(0, EXPERTS) as e:
                        load_expert(e, e, 0)
                    sp.wait_ge(extra_ok, 1)
                    with sp.Fori(0, EXTRA) as r:
                        e = sp.value_load(extra_id[0:1, bass.ds(r, 1)], min_val=0, max_val=EXPERTS - 1)
                        n = sp.value_load(extra_n[0:1, bass.ds(r, 1)], min_val=0, max_val=T)
                        with sp.If(n > P):
                            load_expert(e, r, EXPERTS)
                for i in range(PLE_CHUNKS):
                    load((l, "ple", i), ple_w[l, i])
            sp.wait_ge(h_ple, KT * DEPTH)
            sp.dma_start(outT, hT[:, :, :]).then_inc(out_done, 16)
            sp.wait_ge(out_done, 16)

        def split_phase(eng, l, first, end):
            if phase_q[(l, first)]:
                eng.wait_ge(split_ok, phase_q[(l, first)])
            for g in range(phase_q[(l, first)], phase_q[(l, end)]):
                split_lo(eng, g)

        class Line:

            def __init__(self, eng, split):
                self.eng, self.split, self.n = eng, split, 0

            def to(self, end):
                for g in range(self.n, min(end, len(quarters))):
                    if quarters[g] is None:
                        return
                    self.split(self.eng, g)
                    self.n = g + 1

        @block.gpsimd
        def _(pool):
            pool.memset(ident[:, :], 0.0).then_inc(pool_step, 1)
            pool.memset(flip[:, :], 0.0).then_inc(pool_step, 1)
            pool.memset(ones[:, :], 1.0).then_inc(consts, 1)
            pool.wait_ge(pool_step, 2)
            pool.affine_select(out=flip[:, :], in_=flip[:, :], compare_op=ALU.not_equal, fill=1.0,
                               base=-(P - 1), pattern=[[1, P]], channel_multiplier=1).then_inc(consts, 1)
            pool.affine_select(out=ident[:, :], in_=ident[:, :], compare_op=ALU.not_equal, fill=1.0,
                               base=0, pattern=[[-1, P]], channel_multiplier=1).then_inc(ident_ok, 1)
            split_phase(pool, 0, "mix", "ffn")
            split_phase(pool, 1, "mix", "ffn")
            pool.wait_ge(h_mixed, KT * DEPTH)
            pool.memset(before, 1.0).then_inc(pool_step, 1)
            pool.iota(iota_i, pattern=[[1, P]], base=0, channel_multiplier=0).then_inc(pool_step, 1)
            pool.iota(pick_wi, pattern=[[-1, EXPERTS]], base=EXPERTS, channel_multiplier=0).then_inc(pool_step, 1)
            pool.wait_ge(pool_step, 5)
            pool.affine_select(out=before, in_=before, compare_op=ALU.is_gt, fill=0.0,
                               base=0, pattern=[[1, P]], channel_multiplier=-1).then_inc(pool_route, 1)
            pool.tensor_copy(iota_f, iota_i).then_inc(pool_route, 1)
            pool.tensor_copy(pick_w, pick_wi).then_inc(pool_route, 1)

        @block.scalar
        def _(act):
            act.dma_start(rel[:, :], relT).then_inc(rel_in, 16)
            act.dma_start(row[:, :], rows).then_inc(rows_in, 16)
            def norm(n):
                for q in range(4):
                    wait_h(act, n, q)
                    act.activation(squares[:, 2 * q:2 * q + 2, :], hT[:, 2 * q:2 * q + 2, :], ACT.Square).then_inc(squared, 1)
                if n == 0:
                    act.wait_ge(eps_ok, 1)
                if n == 3 * (n // 3) + 1 and n // 3 % 2:
                    act.dma_start(rw, router_d).then_inc(router_in, 16)
                act.activation(small[:, 65:66], eps_col, ACT.Sqrt)
                act.wait_ge(summed, n + 1)
                act.activation(rms, misc[:, 0:T], ACT.Sqrt, bias=eps_col[:, 0:1], scale=1.0 / D).then_inc(rooted, 1)

            eps_col = small[:, 64:65]

            def qk_norm(l):
                for i in range(6):
                    c, tt = i // 2, i % 2
                    n = 512 if c < 2 else 256
                    hi.to(phase_q[(l, "mix")] + 4 * c + 9)
                    wait_full(act, l, "qkv", c, tt)
                    if i >= 2:
                        act.wait_ge(qk_summed, 6 * l + i - 1)
                    if c == 2:
                        act.activation(v_sb[:, tt, :], work[place[(l, "qkv", c, tt)][0]][:, 256:512], ACT.Copy)
                    act.activation(sqs[:, i % 2, 0:n], bank_of(l, "qkv", c, tt)[:, 0:n], ACT.Square).then_inc(qk_squared, 1)
                    act.wait_ge(qk_summed, 6 * l + i + 1)
                    act.activation(small[:, 8 * (i % 2) + 16:8 * (i % 2) + 16 + n // HD],
                                   small[:, 8 * (i % 2):8 * (i % 2) + n // HD],
                                   ACT.Sqrt, bias=eps_col, scale=1.0 / HD).then_inc(qk_rooted, 1)

            def qk_turns(l):
                for i in range(6):
                    act.wait_ge(qk_turned, 6 * l + i + 1)
                    src = turn_ps[i].rearrange("p (j n) -> p j n", j=4)
                    if i < 4:
                        c, tt = i // 2, i % 2
                        dst = qT[:, 4 * c:4 * c + 4, tt * P:(tt + 1) * P]
                    else:
                        dst = kTT[:, :, (i - 4) * P:(i - 3) * P]
                    act.activation(dst, src, ACT.Copy).then_inc(qkT_ok, 1)

            def evacuate(l, name, j, dst):
                wait_full(act, l, name, j)
                taken(act.activation(dst, bank_of(l, name, j)[:, 0:T], ACT.Copy), l, name, j)

            def exps(l, u):
                g = PAIRS * TT * l + u
                b, t = divmod(u, PAIRS)
                w = P * (b + 1)
                act.wait_ge(max_ok, g + 1)
                m = 32 + 8 * (u % 2)
                for hh in range(2):
                    e = ebuf[:, u % 2, hh, 0:w]
                    act.activation(e, e, ACT.Exp, bias=small[:, m + 2 + hh:m + 3 + hh],
                                   accum_out=small[:, m + 6 + hh:m + 7 + hh])
                act.activation(small[:, m + 4:m + 6], small[:, m + 4:m + 6], ACT.Exp).then_inc(exped, 1)

            def probsT(l, u):
                g = PAIRS * TT * l + u
                w = P * (u // PAIRS + 1)
                act.wait_ge(probs_turned, g + 1)
                if u >= 2:
                    act.wait_ge(pv_done, g - 1)
                act.activation(ptb[:, u % 2, :, 0:w],
                               acc[1][:, 512 * (u % 2):512 * (u % 2) + 512].rearrange("p (h s) -> p h s", h=2)[:, :, 0:w],
                               ACT.Copy).then_inc(probsT_ok, 1)

            def take_pv(l, u):
                g = PAIRS * TT * l + u
                b, t = divmod(u, PAIRS)
                act.wait_ge(pv_done, g + 1)
                act.activation(yaT[:, t, b * P:(b + 1) * P], (pv_ps, misc)[u % 2][:, 0:P],
                               ACT.Copy).then_inc(pv_taken, 1)

            def gates(l):
                act.wait_ge(work_free[place[(l, "ga", KT - 1)][0]], place[(l, "ga", KT - 1)][1] + 1)
                act.wait_ge(work_free[place[(l, "ga", KT - 2)][0]], place[(l, "ga", KT - 2)][1] + 1)
                act.activation(gate_a[:, :, :], gate_a[:, :, :], ACT.Sigmoid).then_inc(sig_ga, 1)
                for c in range(KT):
                    act.wait_ge(ri_done, KT * l + c + 1)
                    act.activation(rT[:, c, :], quad[c % 4][:, 0:T], ACT.Sigmoid, bias=col[:, C_RG + l, c:c + 1])
                    act.activation(lru[:, c, CONV - 1:], quad[c % 4][:, T:2 * T], ACT.Sigmoid,
                                   bias=col[:, C_IG + l, c:c + 1]).then_inc(sig_ri, 1)
                act.activation(gate_b[:, :, :], gate_b[:, :, :], ACT.Sigmoid).then_inc(sig_gb, 1)
                for c in range(KT):
                    if c % 2:
                        hi.to(phase_q[(l, "mix")] + 41 + c // 2 + 1)
                    act.wait_ge(sig_ri, KT * l + c + 1)
                    act.activation(decayT[:, c, :], rT[:, c, :], ACT.Exp, scale=decay[:, 1, l, c:c + 1]).then_inc(decay_ok, 1)
                    act.activation(rT[:, c, :], rT[:, c, :], ACT.Tanh, scale=decay[:, 2, l, c:c + 1]).then_inc(tanh_ok, 1)
                for c in range(KT):
                    act.wait_ge(tanh_ok, KT * l + c + 1)
                    act.activation(rT[:, c, :], rT[:, c, :], ACT.Sqrt).then_inc(sqrt_ok, 1)

            def mixer(l):
                qk_norm(l)
                order = [("lx", j) for j in range(KT)] + [("gb", j) for j in range(KT)] + [("ga", j) for j in range(KT)]
                for g, (name, j) in enumerate(order):
                    dst = {"lx": lru[:, j, CONV - 1:], "gb": gate_b[:, j, :], "ga": gate_a[:, j, :]}[name]
                    hi.to(phase_q[(l, "mix")] + 12 + g + 5)
                    evacuate(l, name, j, dst)
                    if l == 0 and g < FIRST_UNIT:
                        for i in (2 * g, 2 * g + 1):
                            act.wait_ge(flipped, i + 1)
                            act.activation(bias[:, 2 * i:2 * i + 2, :], turn_ps[i % 2].rearrange("p (h s) -> p h s", h=2),
                                           ACT.Copy).then_inc(bias_ok, 1)
                    s = g - FIRST_UNIT
                    if g == FIRST_UNIT - 1:
                        qk_turns(l)
                    if 0 <= s - 2 < UNITS:
                        probsT(l, s - 2)
                    if 0 <= s - 3 < UNITS:
                        take_pv(l, s - 3)
                    if 0 <= s < UNITS:
                        exps(l, s)
                hi.to(phase_q[(l, "mix")] + 36 + 5)
                gates(l)
                for j in range(KT):
                    hi.to(phase_q[(l, "mix")] + 44 + j + 5)
                    wait_full(act, l, "lg", j)
                    ins = act.activation(glgT[:, j, :], bank_of(l, "lg", j)[:, 0:T], ACT.Gelu_apprx_tanh)
                    taken(ins, l, "lg", j)
                hi.to(phase_q[(l, "ffn")] + 5)

            def dense(l):
                for i in range(FC * FT):
                    c, ft = divmod(i, FT)
                    last = q_at[((l, "w3", c), ft)]
                    hi.to(last + 5)
                    wait_full(act, l, "ffn", c, ft)
                    if i >= 2:
                        act.wait_ge(hid_read, FC * FT * (l // 2) + i - 1)
                    act.activation(silu_buf[:, i % 2, :], bank_of(l, "ffn", c, ft)[:, 0:T], ACT.Silu).then_inc(silu_ok, 1)
                    hi.to(last + 7)
                hi.to(phase_q[(l, "ple")] + 5)

            def ple(l):
                for j in range(KT):
                    hi.to(phase_q[(l, "ple")] + j + 5)
                    wait_full(act, l, "ple", j)
                    if j >= 2:
                        act.wait_ge(h_ple, KT * l + j - 1)
                    act.activation(silu_buf[:, j % 2, :], bank_of(l, "ple", j)[:, 0:T], ACT.Sigmoid).then_inc(ple_gate, 1)

            def take_gathered(n):
                for half in range(2):
                    act.wait_ge(m_gathered, n * 2 + (half + 1))
                    act.activation(xg_hi[:, 4 * half:4 * half + 4, :], work[half][:, :].rearrange("p (k n) -> p k n", k=4),
                                   ACT.Copy).then_inc(m_xg_hi, 1)

            def take_y(j):
                act.wait_ge(part_used, j * JOB_Q + UNITS_HELD)
                act.activation(y_sb, acc[0][:, :], ACT.Copy).then_inc(m_y, 1)

            def job(j, first):
                def hi_m(i):
                    n = moe_chunk + first * FFN_CHUNKS + i // 4
                    if i % 4 == 0:
                        act.wait_ge(slot_full[n % RING], j * (16 * FFN_CHUNKS // RING) + 16 * (n // RING + 1))
                    act.wait_ge(part_used, j * JOB_Q + (first * JOB_Q + i + 1))
                    u = (4 * moe_chunk + i) % UNITS_HELD
                    act.activation(w_hi[u][:, :], raw[n % RING][:, (i % 4) * QUARTER:(i % 4 + 1) * QUARTER],
                                   ACT.Copy).then_inc(hi_ok, 1)

                def silu(c):
                    act.wait_ge(part_used, j * JOB_Q + (first * JOB_Q + UNITS_HELD + M_W1[c] + 1))
                    if c:
                        act.wait_ge(m_hid_ok, j * FC + (first * FC + c))
                    act.activation(m_silu, work[0][:, :], ACT.Silu).then_inc(m_silu_ok, 1)

                def turn(c):
                    act.wait_ge(m_turned, j * FC + (first * FC + c + 1))
                    act.activation(hidT_hi, pv_ps[:, :].rearrange("p (f n) -> p f n", f=FT), ACT.Copy).then_inc(m_hidT_hi, 1)

                for i in range(JOB_Q):
                    hi_m(i)
                    if i == AHEAD - 1:
                        take_y(j + first)
                    if i == M_GT + AHEAD - 1:
                        act.wait_ge(m_gturned, j + (first + 1))
                        act.activation(m_gpickT, misc[:, 0:T], ACT.Copy).then_inc(m_gtaken, 1)
                    for c in range(FC):
                        if i == M_W1[c] + AHEAD:
                            silu(c)
                        if i == M_TURN[c] + AHEAD:
                            turn(c)
                take_gathered(j + (first + 1))

            def skipped(r):
                act.wait_ge(m_xg_hi, r * 2 + (2 * EXPERTS + 2))
                for s in range(RING):
                    act.sem_inc(slot_full[s], 16 * FFN_CHUNKS // RING)
                act.sem_inc(hi_ok, JOB_Q)
                act.sem_inc(m_silu_ok, FC)
                act.sem_inc(m_hidT_hi, FC)
                act.sem_inc(m_y, 1)
                act.sem_inc(m_gtaken, 1)
                act.sem_inc(m_xg_hi, 2)

            def moe(l):
                for i in range(4):
                    act.wait_ge(tok_turned, i + 1)
                    tt, half = divmod(i, 2)
                    act.activation(xn_tok[:, tt, half * 512:(half + 1) * 512], quad[i], ACT.Copy).then_inc(tok_ok, 1)
                act.wait_ge(route_diff, 1)
                act.activation(rsmall[:, 3, :], rsmall[:, 2, :], ACT.Exp).then_inc(route_exp, 1)
                take_gathered(0)
                with act.Fori(0, EXPERTS) as e:
                    job(e, 0)
                act.wait_ge(extra_ok, 1)
                with act.Fori(0, EXTRA) as r:
                    n = act.value_load(extra_n[0:1, bass.ds(r, 1)], min_val=0, max_val=T)
                    with act.If(n <= P):
                        skipped(r)
                    with act.Else():
                        job(r, EXPERTS)
                take_y(JOBS)
                hi.n = phase_q[(l, "ple")]
                hi.to(phase_q[(l, "ple")] + 3)

            hi = Line(act, split_hi)
            norm(0)
            act.wait_ge(line_ok, 1)
            act.dma_start(bias_line.ap(), u_line).then_inc(line_out, 16)
            hi.to(UNITS_HELD)
            act.wait_ge(line_out, 16)
            for half in range(2):
                act.dma_start(bands[half], bass.AP(bias_line, half * (HEADS // 2) * U_LEN,
                                                   [[1, P], [U_LEN, HEADS // 2], [1, BAND]])).then_inc(band_in, 16)
            act.wait_ge(abs_lam, 1)
            act.activation(decay[:, 1, :, :], decay[:, 0, :, :], ACT.Exp, scale=-1.0).then_inc(exp_lam, 1)
            for l in range(DEPTH):
                if l:
                    norm(3 * l)
                mixer(l)
                norm(3 * l + 1)
                dense(l) if l % 2 == 0 else moe(l)
                norm(3 * l + 2)
                ple(l)

        @block.tensor
        def _(pe):
            def group_open(l, *g):
                b, n = place[(l, *g)]
                if n:
                    pe.wait_ge(work_free[b], n)
                return work[b]

            def group_close(ins, l, *g):
                ins.then_inc(work_full[place[(l, *g)][0]], 1)

            def need(g):
                pe.wait_ge(split_ok, g + 1)

            def split_product(out, stat, move, start, stop):
                pe.matmul(out, stat[0], move[0], start=start, stop=False, skip_group_check=True)
                pe.matmul(out, stat[0], move[1], start=False, stop=False, skip_group_check=True)
                return pe.matmul(out, stat[1], move[0], start=False, stop=stop, skip_group_check=True)

            def norm(n):
                for k in range(KT):
                    if k % 2 == 0:
                        pe.wait_ge(squared, 4 * n + k // 2 + 1)
                    mm = pe.matmul(misc[:, 0:T], ones[:, :], squares[:, k, :], start=(k == 0), stop=(k == KT - 1))
                mm.then_inc(summed, 1)

            def product(l, name, j, src, wait_src=None):
                g = phase_q[(l, "mix")] + 4 * MIX_AT[name] + j
                out = group_open(l, name, j)
                need(g)
                for k in range(KT):
                    if wait_src is not None:
                        wait_src(k)
                    mm = split_product(out[:, 0:T], (unit(w_hi, g)[:, k, :], unit(w_lo, g)[:, k, :]),
                                       (src[0][:, k, :], src[1][:, k, :]), k == 0, k == KT - 1)
                group_close(mm, l, name, j)

            def qkv(l):
                for c in range(3):
                    out = [group_open(l, "qkv", c, tt) for tt in range(TT)]
                    for q in range(4):
                        g = phase_q[(l, "mix")] + 4 * c + q
                        need(g)
                        w = [part[g % UNITS_HELD][:, :].rearrange("p (k n) -> p k n", k=2) for part in (w_hi, w_lo)]
                        for kk in range(2):
                            k = 2 * q + kk
                            if c == 0:
                                pe.wait_ge(normed, KT * 3 * l + k + 1)
                            for tt in range(TT):
                                mm = split_product(out[tt][:, :], (xn_hi[:, k, tt * P:(tt + 1) * P], xn_lo[:, k, tt * P:(tt + 1) * P]),
                                                   (w[0][:, kk, :], w[1][:, kk, :]), k == 0, k == KT - 1)
                                if k == KT - 1:
                                    group_close(mm, l, "qkv", c, tt)
                        if q < 3:
                            mm.then_inc(rows_used, 1)

            def flip_bias(parts):
                pe.wait_ge(band_in, 32)
                for i in parts:
                    if i >= 2:
                        pe.wait_ge(bias_ok, i - 1)
                    pe.matmul(turn_ps[i % 2], flip[:, :], bands[i // 4][:, 2 * (i % 4):2 * (i % 4) + 2, :],
                              start=True, stop=True).then_inc(flipped, 1)

            def turn_qk(l):
                pe.wait_ge(bias_ok, 8)
                for i in range(6):
                    pe.wait_ge(qk_normed, 6 * l + i + 1)
                    for j in range(4):
                        if i < 4:
                            c, tt = i // 2, i % 2
                            src = q_tok[:, tt, (4 * c + j) * P:(4 * c + j + 1) * P]
                        else:
                            src = k_dup2[:, i - 4, j, :]
                        mm = pe.transpose(turn_ps[i][:, j * P:(j + 1) * P], src, ident[:, :])
                    mm.then_inc(qk_turned, 1)

            def scores(l, u):
                g = UNITS * l + u
                b, t = divmod(u, PAIRS)
                w = P * (b + 1)
                if u == 0:
                    pe.wait_ge(qkT_ok, 6 * (l + 1))
                if u:
                    pe.wait_ge(biased, g)
                for hh in range(2):
                    mm = pe.matmul(score_ps[:, hh, 0:w],
                                   qT[HD * hh:HD * hh + HD, t, b * P:(b + 1) * P],
                                   kTT[HD * hh:HD * hh + HD, t // 2, 0:w], start=True, stop=True)
                mm.then_inc(scored, 1)

            def turn_probs(l, u):
                g = UNITS * l + u
                pe.wait_ge(probs_ok, g + 1)
                if u >= 2:
                    pe.wait_ge(probsT_ok, g - 1)
                for hh in range(2):
                    for kt in range(u // PAIRS + 1):
                        o = 512 * (u % 2) + BAND * hh + P * kt
                        mm = pe.transpose(acc[1][:, o:o + P], ebuf[:, u % 2, hh, P * kt:P * kt + P], ident[:, :])
                mm.then_inc(probs_turned, 1)

            def values(l, u):
                g = UNITS * l + u
                b, t = divmod(u, PAIRS)
                kv = t // 2
                pe.wait_ge(probsT_ok, g + 1)
                if u >= 2:
                    pe.wait_ge(pv_taken, g - 1)
                for hh in range(2):
                    for kt in range(b + 1):
                        mm = pe.matmul((pv_ps, misc)[u % 2][HD * hh:HD * hh + HD, 0:P],
                                       v_sb[:, kt, kv * HD:(kv + 1) * HD], ptb[:, u % 2, hh, P * kt:P * kt + P],
                                       start=(kt == 0), stop=(kt == b))
                mm.then_inc(pv_done, 1)

            def recurrence_gates(l):
                pe.wait_ge(gates_in, 32 * (l + 1))
                for c in range(KT):
                    pe.wait_ge(conv_done, KT * l + c + 1)
                    if c >= 4:
                        pe.wait_ge(sig_ri, KT * l + c - 3)
                    for n, w in enumerate((wrg, wig)):
                        for b in range(2):
                            mm = pe.matmul(quad[c % 4][HD * b:HD * b + HD, T * n:T * n + T],
                                           w[HD * b:HD * b + HD, c, :], xcT[HD * b:HD * b + HD, c, :],
                                           start=True, stop=True)
                    mm.then_inc(ri_done, 1)

            def mixer(l):
                qkv(l)
                order = [(name, j) for name in ("lx", "gb", "ga") for j in range(KT)]
                for g, (name, j) in enumerate(order):
                    product(l, name, j, (xn_hi, xn_lo))
                    if l == 0 and g < FIRST_UNIT:
                        flip_bias((2 * g, 2 * g + 1))
                    s = g - FIRST_UNIT
                    if g == FIRST_UNIT - 1:
                        turn_qk(l)
                    if 0 <= s < UNITS:
                        scores(l, s)
                    if 0 <= s - 2 < UNITS:
                        turn_probs(l, s - 2)
                    if 0 <= s - 3 < UNITS:
                        values(l, s - 3)
                recurrence_gates(l)
                for j in range(KT):
                    product(l, "pa", j, (ya_hi, ya_lo), (lambda k: pe.wait_ge(ya_split, KT * l + k + 1)) if j == 0 else None)
                for j in range(KT):
                    product(l, "lg", j, (xn_hi, xn_lo))
                for j in range(KT):
                    product(l, "pb", j, (yb_hi, yb_lo), (lambda k: pe.wait_ge(yb_ok, KT * l + k + 1)) if j == 0 else None)
                for j in range(KT):
                    product(l, "out", j, (merged_hi, merged_lo),
                            (lambda k: pe.wait_ge(merged, KT * l + k + 1)) if j == 0 else None)

            def dense(l):
                def down(c):
                    pe.wait_ge(hid_ok, FC * FT * (l // 2) + FT * (c + 1))
                    for ft in range(FT):
                        g = q_at[((l, "w2", c), ft)]
                        need(g)
                        hi, lo = unit(w_hi, g), unit(w_lo, g)
                        for j in range(KT):
                            mm = split_product(quad[j // 2][:, T * (j % 2):T * (j % 2) + T], (hi[:, j, :], lo[:, j, :]),
                                               (hid_hi[:, c % 2, ft, :], hid_lo[:, c % 2, ft, :]),
                                               c == 0 and ft == 0 and j % 2 == 0, c == FC - 1 and ft == FT - 1)
                        mm.then_inc(ffn_acc, 1)

                for c in range(FC):
                    for ft in range(FT):
                        out = group_open(l, "ffn", c, ft)
                        for half, w in enumerate(("w1", "w3")):
                            g = q_at[((l, w, c), ft)]
                            need(g)
                            hi, lo = unit(w_hi, g), unit(w_lo, g)
                            for k in range(KT):
                                if c == 0 and ft == 0 and half == 0:
                                    pe.wait_ge(normed, KT * (3 * l + 1) + k + 1)
                                mm = split_product(out[:, T * half:T * half + T], (hi[:, k, :], lo[:, k, :]),
                                                   (xn_hi[:, k, :], xn_lo[:, k, :]), k == 0, k == KT - 1)
                        group_close(mm, l, "ffn", c, ft)
                    if c:
                        down(c - 1)
                down(FC - 1)

            def ple(l):
                n = 3 * l + 2
                pe.wait_ge(ple_in, 32 * (l + 1))
                for j in range(KT):
                    out = group_open(l, "ple", j)
                    for k in range(2):
                        pe.matmul(out[:, T:2 * T], wpp[:, k, j * P:(j + 1) * P], p_sb[:, k, :], start=(k == 0), stop=(k == 1))
                    g = phase_q[(l, "ple")] + j
                    need(g)
                    hi, lo = unit(w_hi, g), unit(w_lo, g)
                    for k in range(KT):
                        if j == 0:
                            pe.wait_ge(normed, KT * n + k + 1)
                        mm = split_product(out[:, 0:T], (hi[:, k, :], lo[:, k, :]), (xn_hi[:, k, :], xn_lo[:, k, :]),
                                           k == 0, k == KT - 1)
                    group_close(mm, l, "ple", j)

            def gather(n):
                pe.wait_ge(m_built, n + 1)
                for half in range(2):
                    for kk in range(4):
                        k = 4 * half + kk
                        for tt in range(TT):
                            mm = pe.matmul(work[half][:, kk * P:(kk + 1) * P], xn_tok[:, tt, k * P:(k + 1) * P],
                                           m_pick[:, tt, :], start=(tt == 0), stop=(tt == TT - 1))
                    mm.then_inc(m_gathered, 1)

            def combine(n):
                pe.wait_ge(m_y, n + 1)
                pe.wait_ge(m_gtaken, n + 1)
                for q in range(4):
                    if q >= 2:
                        pe.wait_ge(m_added, n * 4 + (q - 1))
                    for kk in range(2):
                        k = 2 * q + kk
                        mm = pe.matmul((pv_ps, misc)[q % 2][:, T * kk:T * kk + T], y_sb[:, k * P:(k + 1) * P],
                                       m_gpickT, start=True, stop=True)
                    mm.then_inc(m_combined, 1)

            def job(j, first):
                def part(i, k):
                    pe.wait_ge(split_ok, j * JOB_Q + (4 * moe_chunk + first * JOB_Q + i + 1))
                    u = (4 * moe_chunk + i) % UNITS_HELD
                    return [p[u][:, :].rearrange("p (k n) -> p k n", k=k) for p in (w_hi, w_lo)]

                def up(half, c):
                    if c == 0 and half == 0:
                        pe.wait_ge(m_xg, j * 2 + (2 * first + 2))
                    if c:
                        pe.wait_ge((m_silu_ok, m_hid_ok)[half], j * FC + (first * FC + c))
                    for q in range(4):
                        w = part(4 * FFN_AT[(("w1", "w3")[half], c)] + q, 2)
                        for kk in range(2):
                            k = 2 * q + kk
                            mm = split_product(work[half][:, :], (xg_hi[:, k, :], xg_lo[:, k, :]),
                                               (w[0][:, kk, :], w[1][:, kk, :]), k == 0, k == KT - 1)
                        mm.then_inc(part_used, 1)

                def turn(c):
                    pe.wait_ge(m_hid_ok, j * FC + (first * FC + c + 1))
                    if c:
                        pe.wait_ge(m_hidT, j * FC + (first * FC + c))
                    else:
                        pe.wait_ge(m_added, j * 4 + (4 * first + 3))
                    for ft in range(FT):
                        mm = pe.transpose(pv_ps[:, ft * P:(ft + 1) * P], m_hid[:, ft * P:(ft + 1) * P], ident[:, :])
                    mm.then_inc(m_turned, 1)

                def down(c):
                    pe.wait_ge(m_hidT, j * FC + (first * FC + c + 1))
                    for ft in range(FT):
                        w = part(4 * FFN_AT[("w2", c)] + ft, 2)
                        for half in range(2):
                            mm = split_product(acc[0][:, 512 * half:512 * half + 512], (hidT_hi[:, ft, :], hidT_lo[:, ft, :]),
                                               (w[0][:, half, :], w[1][:, half, :]),
                                               c == 0 and ft == 0, c == FC - 1 and ft == FT - 1)
                        mm.then_inc(part_used, 1)

                for c in range(FC + 1):
                    if c < FC:
                        up(0, c)
                    if c == 0:
                        combine(j + first)
                    else:
                        turn(c - 1)
                    if c < FC:
                        up(1, c)
                    else:
                        gather(j + (first + 1))
                    if c == 0:
                        pe.wait_ge(m_added, j * 4 + (4 * first + 4))
                        for tt in range(TT):
                            mm = pe.transpose(misc[:, tt * P:(tt + 1) * P], m_gpick[:, tt, :], ident[:, :])
                        mm.then_inc(m_gturned, 1)
                    else:
                        down(c - 1)

            def skipped(r):
                pe.wait_ge(part_used, r * JOB_Q + (EXPERTS * JOB_Q + UNITS_HELD))
                pe.sem_inc(part_used, JOB_Q)
                pe.sem_inc(m_gathered, 2)
                pe.sem_inc(m_turned, FC)
                pe.sem_inc(m_combined, 4)
                pe.sem_inc(m_gturned, 1)

            def moe(l):
                pe.wait_ge(router_in, 16)
                for tt in range(TT):
                    for k in range(KT):
                        if tt == 0:
                            pe.wait_ge(normed, KT * (3 * l + 1) + k + 1)
                        mm = pe.matmul(misc[:, 8 * tt:8 * tt + 8], xnT[:, k, tt * P:(tt + 1) * P], rw[:, k, :],
                                       start=(k == 0), stop=(k == KT - 1))
                mm.then_inc(logits_done, 1)
                for i in range(4):
                    tt, half = divmod(i, 2)
                    for kk in range(4):
                        mm = pe.transpose(quad[i][:, kk * P:(kk + 1) * P],
                                          xnT[:, 4 * half + kk, tt * P:(tt + 1) * P], ident[:, :])
                    mm.then_inc(tok_turned, 1)
                pe.wait_ge(route_masks, 1)
                pe.wait_ge(pool_route, 3)
                mk = route[:, M_MASK, :, :]
                pe.matmul(misc[:, 64:72], before, mk[:, 0, :], start=True, stop=True)
                pe.matmul(misc[:, 72:80], ones[:, :], mk[:, 0, :], start=True, stop=False)
                pe.matmul(misc[:, 72:80], before, mk[:, 1, :], start=False, stop=True)
                pe.matmul(misc[:, 80:88], ones[:, :], mk[:, 0, :], start=True, stop=False)
                pe.matmul(misc[:, 80:88], ones[:, :], mk[:, 1, :], start=False, stop=True).then_inc(ranked, 1)
                pe.wait_ge(tok_ok, 4)
                wait_full(pe, l, "out", KT - 1)
                pe.sem_inc(part_used, UNITS_HELD)
                pe.wait_ge(counts_ok, 1)
                gather(0)
                with pe.Fori(0, EXPERTS) as e:
                    job(e, 0)
                pe.wait_ge(extra_ok, 1)
                with pe.Fori(0, EXTRA) as r:
                    n = pe.value_load(extra_n[0:1, bass.ds(r, 1)], min_val=0, max_val=T)
                    with pe.If(n <= P):
                        skipped(r)
                    with pe.Else():
                        job(r, EXPERTS)
                combine(JOBS)

            pe.wait_ge(consts, 2)
            norm(0)
            pe.wait_ge(ident_ok, 1)
            for l in range(DEPTH):
                if l:
                    norm(3 * l)
                mixer(l)
                norm(3 * l + 1)
                dense(l) if l % 2 == 0 else moe(l)
                norm(3 * l + 2)
                ple(l)

        @block.vector
        def _(dve):
            step = Steps(dve, dve_step)

            def split_pair(full, hi, lo, k, done):
                step.settle()
                step(dve.tensor_copy(hi[:, k:k + 2, :], full[:, k:k + 2, :]))
                step.settle()
                dve.tensor_tensor(lo[:, k:k + 2, :], full[:, k:k + 2, :], hi[:, k:k + 2, :].bitcast(F32),
                                  ALU.subtract).then_inc(done, 2)

            def bias_lines():
                step(dve.memset(u_line, MASKED))
                step(dve.memset(u_zero, 0.0))
                dve.wait_ge(rel_in, 16)
                step.settle()
                for b in range(BUCKETS):
                    dists = [d for d in range(WINDOW) if bucket_of(d) == b]
                    if not dists:
                        continue
                    j0, j1 = BAND - 1 - dists[-1], BAND - dists[0]
                    step(dve.tensor_scalar(u_line[:, j0:j1], u_zero[:, 0:j1 - j0], rel[:, b:b + 1], None, ALU.add))
                step.settle()
                dve.sem_inc(line_ok, 1)

            def decays():
                lam = col[:, C_LAM:C_LAM + DEPTH, :]
                y, z, q = decay[:, 1, :, :], decay[:, 2, :, :], decay[:, 0, :, :]
                t2 = small[:, 66:82].rearrange("p (l k) -> p l k", l=DEPTH)
                step(dve.tensor_scalar(z, lam, -1.0, None, ALU.mult))
                step.settle()
                dve.tensor_tensor(decay[:, 0, :, :], lam, z, ALU.max).then_inc(abs_lam, 1)
                dve.wait_ge(exp_lam, 1)
                step(dve.tensor_scalar(z, y, 2.0, None, ALU.add))
                step.settle()
                step(dve.reciprocal(t2, z))
                step.settle()
                step(dve.tensor_tensor(z, y, t2, ALU.mult))
                step.settle()
                step(dve.tensor_tensor(t2, z, z, ALU.mult))
                step.settle()
                step(dve.tensor_scalar(q, t2, 1.0 / 21, None, ALU.mult))
                for n in range(9, 0, -1):
                    step.settle()
                    step(dve.scalar_tensor_tensor(out=q, in0=q, scalar=1.0 / (2 * n + 1), in1=t2, op0=ALU.add, op1=ALU.mult))
                step.settle()
                step(dve.scalar_tensor_tensor(out=q, in0=q, scalar=1.0, in1=z, op0=ALU.add, op1=ALU.mult))
                step(dve.tensor_scalar(t2, lam, -1.0, 0.0, ALU.mult, ALU.max))
                step.settle()
                step(dve.scalar_tensor_tensor(out=t2, in0=q, scalar=2.0, in1=t2, op0=ALU.mult, op1=ALU.add))
                step.settle()
                step(dve.tensor_scalar(decay[:, 1, :, :], t2, -LRU_C, None, ALU.mult))
                step(dve.tensor_scalar(decay[:, 2, :, :], t2, LRU_C / 2, None, ALU.mult))
                dve.wait_ge(rows_in, 16)
                step(dve.tensor_scalar(row[:, R_Q:R_Q + DEPTH * HD], row[:, R_Q:R_Q + DEPTH * HD], HD ** -0.5, None, ALU.mult))
                step.settle()

            def norm(n):
                gain = col[:, (C_MIX, C_FFN, C_PLE)[n % 3] + n // 3, :]
                dve.wait_ge(rooted, n + 1)
                step(dve.reciprocal(rinv, rms))
                step.settle()
                if n == 0:
                    dve.wait_ge(small_in, 16)
                routed = n % 3 == 1 and n // 3 % 2 == 1
                for k in range(0, KT, 2):
                    for i in (k, k + 1):
                        ins = dve.scalar_tensor_tensor(out=xnT[:, i, :], in0=hT[:, i, :], scalar=gain[:, i:i + 1], in1=rinv,
                                                       op0=ALU.mult, op1=ALU.mult)
                    if routed:
                        ins.then_inc(normed, 2)
                    else:
                        step(ins)
                        split_pair(xnT, xn_hi, xn_lo, k, normed)

            def qk_norm(l):
                for i in range(6):
                    c, tt = i // 2, i % 2
                    n = 512 if c < 2 else 256
                    h = n // HD
                    b = 8 * (i % 2)
                    dve.wait_ge(qk_squared, 6 * l + i + 1)
                    dve.tensor_reduce(small[:, b:b + h], sqs[:, i % 2, 0:n].rearrange("p (h d) -> p h d", h=h),
                                      AX_X, ALU.add).then_inc(qk_summed, 1)
                    dve.wait_ge(qk_rooted, 6 * l + i + 1)
                    step(dve.reciprocal(small[:, b + 48:b + 48 + h], small[:, b + 16:b + 16 + h]))
                    step.settle()
                    ps = bank_of(l, "qkv", c, tt)[:, 0:n].rearrange("p (h d) -> p h d", h=h)
                    rb = small[:, b + 48:b + 48 + h].unsqueeze(2).to_broadcast([P, h, HD])
                    if c < 2:
                        q = q_tok[:, tt, 512 * c:512 * c + 512].rearrange("p (h d) -> p h d", h=h)
                        gb = row[:, R_Q + HD * l:R_Q + HD * l + HD].unsqueeze(1).to_broadcast([P, h, HD])
                        taken(dve.tensor_tensor(q, ps, rb, ALU.mult), l, "qkv", c, tt)
                        bk, m = place[(l, "qkv", c, tt)]
                        dve.wait_ge(work_free[bk], m + 1)
                        dve.tensor_tensor(q, q, gb, ALU.mult).then_inc(qk_normed, 1)
                    else:
                        kd = k_dup[:, tt, :, :, :]
                        gb = row[:, R_K + HD * l:R_K + HD * l + HD].unsqueeze(1).to_broadcast([P, h, HD])
                        taken(dve.tensor_tensor(kd[:, :, 0, :], ps, rb, ALU.mult), l, "qkv", c, tt)
                        bk, m = place[(l, "qkv", c, tt)]
                        dve.wait_ge(work_free[bk], m + 1)
                        step(dve.tensor_tensor(kd[:, :, 0, :], kd[:, :, 0, :], gb, ALU.mult))
                        step.settle()
                        dve.tensor_copy(kd[:, :, 1, :], kd[:, :, 0, :]).then_inc(qk_normed, 1)

            def add_bias(l, u):
                g = UNITS * l + u
                b, t = divmod(u, PAIRS)
                w = P * (b + 1)
                m = 32 + 8 * (u % 2)
                dve.wait_ge(scored, g + 1)
                if u >= 2:
                    dve.wait_ge(probs_turned, g - 1)
                if l == 0 and u == 0:
                    dve.wait_ge(bias_ok, 8)
                e = ebuf[:, u % 2, :, 0:w]
                dve.tensor_tensor(e, score_ps[:, :, 0:w], bias[:, 2 * t:2 * t + 2, BAND - w:BAND], ALU.add).then_inc(biased, 1)
                dve.wait_ge(biased, g + 1)
                sink = row[:, R_SINK + HEADS * l + 2 * t:R_SINK + HEADS * l + 2 * t + 2]
                step(dve.tensor_reduce(small[:, m:m + 2], e, AX_X, ALU.max))
                step.settle()
                step(dve.tensor_tensor(small[:, m:m + 2], small[:, m:m + 2], sink, ALU.max))
                step.settle()
                dve.tensor_scalar(small[:, m + 2:m + 4], small[:, m:m + 2], -1.0, None, ALU.mult)
                dve.tensor_tensor(small[:, m + 4:m + 6], sink, small[:, m:m + 2], ALU.subtract).then_inc(max_ok, 1)

            def probs(l, u):
                g = UNITS * l + u
                w = P * (u // PAIRS + 1)
                m = 32 + 8 * (u % 2)
                dve.wait_ge(exped, g + 1)
                step(dve.tensor_tensor(small[:, m:m + 2], small[:, m + 4:m + 6], small[:, m + 6:m + 8], ALU.add))
                step.settle()
                step(dve.reciprocal(small[:, m:m + 2], small[:, m:m + 2]))
                step.settle()
                for hh in range(2):
                    e = ebuf[:, u % 2, hh, 0:w]
                    ins = dve.tensor_scalar(e, e, small[:, m + hh:m + hh + 1], None, ALU.mult)
                ins.then_inc(probs_ok, 1)

            def conv(l, c):
                bk, n = place[(l, "lx", c)]
                dve.wait_ge(work_free[bk], n + 1)
                x = lru[:, c, :]
                o = xcT[:, c, :]
                w = [col[:, C_CONV + CONV * l + j, c:c + 1] for j in range(CONV)]
                step(dve.tensor_scalar(o, x[:, 0:T], w[0], col[:, C_CB + l, c:c + 1], ALU.mult, ALU.add))
                for j in range(1, CONV):
                    step.settle()
                    ins = dve.scalar_tensor_tensor(out=o, in0=x[:, j:j + T], scalar=w[j], in1=o, op0=ALU.mult, op1=ALU.add)
                    if j < CONV - 1:
                        step(ins)
                ins.then_inc(conv_done, 1)

            def recurrence(l):
                for c in range(KT):
                    dve.wait_ge(sqrt_ok, KT * l + c + 1)
                    step(dve.scalar_tensor_tensor(out=rT[:, c, :], in0=decayT[:, c, :], scalar=1.0, in1=rT[:, c, :],
                                                  op0=ALU.add, op1=ALU.mult))
                    step.settle()
                    step(dve.tensor_tensor(rT[:, c, :], rT[:, c, :], lru[:, c, CONV - 1:], ALU.mult))
                    step.settle()
                    step(dve.tensor_tensor_scan(xcT[:, c, :], decayT[:, c, :], rT[:, c, :], 0.0, ALU.mult, ALU.add))

            def mixer(l):
                qk_norm(l)
                for g in range(3 * KT):
                    s = g - FIRST_UNIT
                    if 0 <= s - 1 < UNITS:
                        probs(l, s - 1)
                    if 0 <= s < UNITS:
                        add_bias(l, s)
                    if 0 <= g - FIRST_UNIT - 2 < KT:
                        conv(l, g - FIRST_UNIT - 2)
                dve.wait_ge(pv_taken, UNITS * (l + 1))
                for k in range(0, KT, 2):
                    split_pair(yaT, ya_hi, ya_lo, k, ya_split)
                for j in range(KT):
                    wait_full(dve, l, "pa", j)
                    if j == 0:
                        dve.wait_ge(sig_ga, l + 1)
                    taken(dve.tensor_tensor(gate_a[:, j, :], gate_a[:, j, :], bank_of(l, "pa", j)[:, 0:T], ALU.mult), l, "pa", j)
                    dve.wait_ge(sig_ri, KT * l + j + 1)
                    step(dve.tensor_tensor(lru[:, j, CONV - 1:], lru[:, j, CONV - 1:], xcT[:, j, :], ALU.mult))
                recurrence(l)
                step.settle()
                for j in range(KT):
                    bk, n = place[(l, "lg", j)]
                    dve.wait_ge(work_free[bk], n + 1)
                    step(dve.tensor_tensor(xcT[:, j, :], xcT[:, j, :], glgT[:, j, :], ALU.mult))
                    if j % 2:
                        split_pair(xcT, yb_hi, yb_lo, j - 1, yb_ok)
                dve.wait_ge(sig_gb, l + 1)
                for j in range(KT):
                    wait_full(dve, l, "pb", j)
                    taken(dve.tensor_tensor(gate_b[:, j, :], gate_b[:, j, :], bank_of(l, "pb", j)[:, 0:T], ALU.mult), l, "pb", j)
                    bk, n = place[(l, "pb", j)]
                    dve.wait_ge(work_free[bk], n + 1)
                    step(dve.tensor_tensor(gate_a[:, j, :], gate_a[:, j, :], gate_b[:, j, :], ALU.add))
                    if j % 2:
                        split_pair(gate_a, merged_hi, merged_lo, j - 1, merged)
                for j in range(KT):
                    if l % 2 == 0 and j == KT - 1:
                        dve.wait_ge(split_ok, phase_q[(l, "ffn")])
                        lo.n = phase_q[(l, "ffn")]
                        lo.to(lo.n + 2)
                    wait_full(dve, l, "out", j)
                    taken(dve.tensor_tensor(hT[:, j, :], hT[:, j, :], bank_of(l, "out", j)[:, 0:T], ALU.add), l, "out", j)
                    bk, n = place[(l, "out", j)]
                    dve.wait_ge(work_free[bk], n + 1)
                    dve.sem_inc(h_mixed, 1)

            def dense(l):
                for i in range(FC * FT):
                    c, ft = divmod(i, FT)
                    last = q_at[((l, "w3", c), ft)]
                    lo.to(last + 5)
                    dve.wait_ge(silu_ok, FC * FT * (l // 2) + i + 1)
                    s = silu_buf[:, i % 2, :]
                    taken(dve.tensor_tensor(s, s, bank_of(l, "ffn", c, ft)[:, T:2 * T], ALU.mult), l, "ffn", c, ft)
                    bk, n = place[(l, "ffn", c, ft)]
                    dve.wait_ge(work_free[bk], n + 1)
                    step(dve.tensor_copy(hid_hi[:, c % 2, ft, :], s))
                    step.settle()
                    dve.tensor_tensor(hid_lo[:, c % 2, ft, :], s, hid_hi[:, c % 2, ft, :].bitcast(F32),
                                      ALU.subtract).then_inc(hid_ok, 1)
                    dve.wait_ge(hid_ok, FC * FT * (l // 2) + i + 1)
                    dve.sem_inc(hid_read, 1)
                    lo.to(last + 7)
                lo.to(phase_q[(l, "ple")] + 2)
                dve.wait_ge(ffn_acc, FC * FT * (l // 2 + 1))
                for b in range(4):
                    dve.tensor_tensor(hT[:, 2 * b:2 * b + 2, :], hT[:, 2 * b:2 * b + 2, :],
                                      quad[b].rearrange("p (k t) -> p k t", k=2), ALU.add).then_inc(h_ffn, 1)

            def ple(l):
                for j in range(KT):
                    lo.to(phase_q[(l, "ple")] + min(j + 5, KT))
                    wait_full(dve, l, "ple", j)
                    dve.wait_ge(ple_gate, KT * l + j + 1)
                    s = silu_buf[:, j % 2, :]
                    taken(dve.tensor_tensor(s, s, bank_of(l, "ple", j)[:, T:2 * T], ALU.mult), l, "ple", j)
                    bk, n = place[(l, "ple", j)]
                    dve.wait_ge(work_free[bk], n + 1)
                    dve.tensor_tensor(hT[:, j, :], hT[:, j, :], s, ALU.add).then_inc(h_ple, 1)

            def routing():
                count = over[:, 0, :]
                L, EQ, V, MK1, MK2, GT, MK = (route[:, n, :, :] for n in (0, 1, 2, 3, 4, 5, M_MASK))
                m1, m2, df, ex, w1, w2 = (rsmall[:, n, :] for n in range(6))
                mv = rsmall[:, 6, :]

                def wide(a):
                    return a.unsqueeze(2).to_broadcast([P, TT, EXPERTS])

                pw = pick_w.unsqueeze(1).to_broadcast([P, TT, EXPERTS])
                rb = row[:, R_RB:R_RB + EXPERTS].unsqueeze(1).to_broadcast([P, TT, EXPERTS])
                dve.wait_ge(logits_done, 1)
                dve.wait_ge(pool_route, 3)
                step(dve.tensor_tensor(L, misc[:, 0:16].rearrange("p (t e) -> p t e", t=TT), rb, ALU.add))
                step.settle()
                for m, mk in ((m1, MK1), (m2, MK2)):
                    step(dve.tensor_reduce(m, L, AX_X, ALU.max))
                    step.settle()
                    step(dve.tensor_tensor(EQ, L, wide(m), ALU.is_equal))
                    step.settle()
                    step(dve.tensor_tensor(V, EQ, pw, ALU.mult))
                    step.settle()
                    step(dve.tensor_reduce(mv, V, AX_X, ALU.max))
                    step.settle()
                    step(dve.tensor_tensor(mk, V, wide(mv), ALU.is_equal))
                    step.settle()
                    if mk is MK1:
                        step(dve.scalar_tensor_tensor(out=L, in0=mk, scalar=-3e38, in1=L, op0=ALU.mult, op1=ALU.add))
                        step.settle()
                step(dve.tensor_tensor(MK, MK1, MK2, ALU.add))
                step.settle()
                dve.sem_inc(route_masks, 1)
                dve.tensor_tensor(df, m2, m1, ALU.subtract).then_inc(route_diff, 1)
                dve.wait_ge(route_exp, 1)
                step(dve.tensor_scalar(w2, ex, 1.0, None, ALU.add))
                step.settle()
                step(dve.reciprocal(w1, w2))
                step.settle()
                step(dve.tensor_tensor(w2, ex, w1, ALU.mult))
                step(dve.tensor_tensor(MK1, MK1, wide(w1), ALU.mult))
                step.settle()
                step(dve.tensor_tensor(MK2, MK2, wide(w2), ALU.mult))
                step(dve.memset(gate_m, 0.0))
                step(dve.memset(rank_m, -1.0))
                step.settle()
                step(dve.tensor_tensor(gate_m[:, :, 0:EXPERTS], MK1, MK2, ALU.add))
                dve.wait_ge(ranked, 1)
                step(dve.tensor_scalar(GT, misc[:, 64:80].rearrange("p (t e) -> p t e", t=TT), 1.0, None, ALU.add))
                step.settle()
                step(dve.tensor_tensor(GT, GT, MK, ALU.mult))
                step.settle()
                step(dve.tensor_scalar(rank_m[:, :, 0:EXPERTS], GT, -1.0, None, ALU.add))
                step(dve.tensor_copy(count, misc[:, 80:88]))
                step.settle()
                dve.sem_inc(counts_ok, 1)

            def extra_jobs():
                count, pos, sel, ids = (over[:, n, :] for n in range(4))
                sel3 = gaf[:, 1904:1928].rearrange("p (r e) -> p r e", r=EXTRA)
                t24 = gaf[:, 1928:1952].rearrange("p (r e) -> p r e", r=EXTRA)
                t48 = gaf[:, 1856:1904].rearrange("p (r t e) -> p r t e", r=EXTRA, t=TT)
                t6 = gaf[:, 1952:1958].rearrange("p (r t) -> p r t", r=EXTRA)

                def more(table):
                    return table[:, :, EXPERTS:JOBS].rearrange("p t r -> p r t")

                one8 = over[:, 4, :]
                s_id, s_n = over[:, 5, :], over[:, 6, :]
                t16 = route[:, 7, :, :]
                step(dve.tensor_scalar(sel, count, float(P), None, ALU.is_gt))
                step(dve.memset(one8, 1.0))
                step(dve.memset(s_id, 0.0))
                step(dve.memset(s_n, 0.0))
                step.settle()
                step(dve.tensor_tensor_scan(pos, one8, sel, 0.0, ALU.mult, ALU.add))
                step.settle()
                step(dve.tensor_tensor(pos, pos, sel, ALU.mult))
                step.settle()
                for r in range(EXTRA):
                    step(dve.tensor_scalar(sel3[:, r, :], pos, float(r + 1), None, ALU.is_equal))
                step(dve.tensor_scalar(ids, pick_w, -1.0, float(EXPERTS), ALU.mult, ALU.add))
                step(dve.tensor_scalar(t16, rank_m[:, :, 0:EXPERTS], float(1 - P), None, ALU.add))
                step.settle()
                of_tokens = sel3.unsqueeze(2).to_broadcast([P, EXTRA, TT, EXPERTS])
                step(dve.tensor_tensor(t24, sel3, count.unsqueeze(1).to_broadcast([P, EXTRA, EXPERTS]), ALU.mult))
                step(dve.tensor_tensor(t48, t16.unsqueeze(1).to_broadcast([P, EXTRA, TT, EXPERTS]), of_tokens, ALU.mult))
                step.settle()
                step(dve.tensor_reduce(s_n[:, 0:EXTRA], t24, AX_X, ALU.add))
                step(dve.tensor_reduce(t6, t48, AX_X, ALU.add))
                step.settle()
                step(dve.tensor_tensor(t24, sel3, ids.unsqueeze(1).to_broadcast([P, EXTRA, EXPERTS]), ALU.mult))
                step(dve.tensor_scalar(more(rank_m), t6, -1.0, None, ALU.add))
                step(dve.tensor_tensor(t48, gate_m[:, :, 0:EXPERTS].unsqueeze(1).to_broadcast([P, EXTRA, TT, EXPERTS]),
                                       of_tokens, ALU.mult))
                step.settle()
                step(dve.tensor_reduce(s_id[:, 0:EXTRA], t24, AX_X, ALU.add))
                step(dve.tensor_reduce(t6, t48, AX_X, ALU.add))
                step.settle()
                step(dve.tensor_copy(more(gate_m), t6))
                step.settle()
                step(dve.tensor_copy(extra_id, s_id[:, 0:EXTRA]))
                step(dve.tensor_copy(extra_n, s_n[:, 0:EXTRA]))
                step.settle()
                dve.sem_inc(extra_ok, 1)

            def build(n):
                for tt in range(TT):
                    dve.tensor_scalar(m_pick[:, tt, :], iota_f, rank_m[:, tt, bass.ds(n, 1)], None, ALU.is_equal)
                    ins = dve.tensor_scalar(m_gpick[:, tt, :], iota_f, rank_m[:, tt, bass.ds(n, 1)],
                                            gate_m[:, tt, bass.ds(n, 1)], ALU.is_equal, ALU.mult)
                ins.then_inc(m_built, 1)

            def split_gathered(n):
                for half in range(2):
                    dve.wait_ge(m_xg_hi, n * 2 + (half + 1))
                    k = slice(4 * half, 4 * half + 4)
                    dve.tensor_tensor(xg_lo[:, k, :], work[half][:, :].rearrange("p (k n) -> p k n", k=4),
                                      xg_hi[:, k, :].bitcast(F32), ALU.subtract).then_inc(m_xg, 1)

            def add_combined(n):
                for q in range(4):
                    dve.wait_ge(m_combined, n * 4 + (q + 1))
                    dve.tensor_tensor(hT[:, 2 * q:2 * q + 2, :], hT[:, 2 * q:2 * q + 2, :],
                                      (pv_ps, misc)[q % 2][:, :].rearrange("p (k t) -> p k t", k=2),
                                      ALU.add).then_inc(m_added, 1)

            def job(j, first):
                def lo_m(i):
                    n = moe_chunk + first * FFN_CHUNKS + i // 4
                    dve.wait_ge(hi_ok, j * JOB_Q + (4 * moe_chunk + first * JOB_Q + i + 1))
                    u = (4 * moe_chunk + i) % UNITS_HELD
                    dve.tensor_tensor(w_lo[u][:, :], raw[n % RING][:, (i % 4) * QUARTER:(i % 4 + 1) * QUARTER],
                                      w_hi[u][:, :].bitcast(F32), ALU.subtract).then_inc(split_ok, 1)

                for i in range(JOB_Q):
                    lo_m(i)
                    if i == 3 + AHEAD:
                        add_combined(j + first)
                    if i == M_W3[1]:
                        dve.wait_ge(m_gturned, j + (first + 1))
                        build(j + (first + 1))
                    for c in range(FC):
                        if i == M_W3[c] + AHEAD:
                            dve.wait_ge(part_used, j * JOB_Q + (first * JOB_Q + UNITS_HELD + M_W3[c] + 1))
                            dve.wait_ge(m_silu_ok, j * FC + (first * FC + c + 1))
                            dve.tensor_tensor(m_hid, m_silu, work[1][:, :], ALU.mult).then_inc(m_hid_ok, 1)
                        if i == M_TURN[c] + AHEAD:
                            dve.wait_ge(m_hidT_hi, j * FC + (first * FC + c + 1))
                            dve.tensor_tensor(hidT_lo, pv_ps[:, :].rearrange("p (f n) -> p f n", f=FT),
                                              hidT_hi.bitcast(F32), ALU.subtract).then_inc(m_hidT, 1)
                split_gathered(j + (first + 1))

            def skipped(r):
                dve.wait_ge(m_xg, r * 2 + (2 * EXPERTS + 2))
                dve.sem_inc(split_ok, JOB_Q)
                dve.sem_inc(m_xg, 2)
                dve.sem_inc(m_hid_ok, FC)
                dve.sem_inc(m_hidT, FC)
                dve.sem_inc(m_added, 4)
                dve.sem_inc(m_built, 1)

            def moe(l):
                routing()
                step(dve.memset(m_gpickT, 0.0))
                step.settle()
                dve.sem_inc(m_gtaken, 1)
                build(0)
                extra_jobs()
                dve.wait_ge(split_ok, phase_q[(l, "ffn")])
                split_gathered(0)
                with dve.Fori(0, EXPERTS) as e:
                    job(e, 0)
                with dve.Fori(0, EXTRA) as r:
                    n = dve.value_load(extra_n[0:1, bass.ds(r, 1)], min_val=0, max_val=T)
                    with dve.If(n <= P):
                        skipped(r)
                    with dve.Else():
                        job(r, EXPERTS)
                lo.n = phase_q[(l, "ple")]
                lo.to(phase_q[(l, "ple")] + 2)
                add_combined(JOBS)

            lo = Line(dve, split_lo)
            dve.memset(small[:, 64:65], EPS).then_inc(eps_ok, 1)
            step(dve.memset(lru[:, :, 0:CONV - 1], 0.0))
            bias_lines()
            norm(0)
            decays()
            for l in range(DEPTH):
                if l:
                    norm(3 * l)
                mixer(l)
                norm(3 * l + 1)
                dense(l) if l % 2 == 0 else moe(l)
                norm(3 * l + 2)
                ple(l)


def feature_cols(a):
    return a.reshape(-1, KT, P).transpose(2, 0, 1)


def column_chunks(w):
    n = w.shape[1] // CW
    return w.reshape(KT, P, n, CW).transpose(2, 1, 0, 3).reshape(n, P, CHUNK)


def row_chunks(w):
    return w.reshape(FC, FT, P, D).transpose(0, 2, 1, 3).reshape(FC, P, CHUNK)


def ffn_blocks(w1, w3, w2):
    parts = {"w1": column_chunks(w1), "w3": column_chunks(w3), "w2": row_chunks(w2)}
    return [parts[w][c] for w, c in ffn_order()]


def kernel(**inputs):
    import concourse.bacc as _bacc
    from concourse.bass_utils import run_bass_kernel_spmd as _run

    a = {k: np.asarray(v) for k, v in inputs.items()}
    asc = np.ascontiguousarray
    mix = []
    for l in range(DEPTH):
        win = column_chunks(a["w_in"][l])
        mix += [win[c] for c in W_IN_ORDER]
        mix += list(column_chunks(a["w_proj_attn"][l]))
        mix += [win[c] for c in W_IN_LG]
        mix += list(column_chunks(a["w_proj_lru"][l])) + list(column_chunks(a["w_out"][l]))
    moe = []
    for e in range(EXPERTS):
        moe += ffn_blocks(a["moe_w1"][0, e], a["moe_w3"][0, e], a["moe_w2"][0, e])
    cols = np.concatenate([
        a["mix_norm"], a["ffn_norm"], a["ple_norm"], a["conv_w"].reshape(DEPTH * CONV, D), a["conv_b"],
        a["b_rg"].reshape(DEPTH, D), a["b_ig"].reshape(DEPTH, D), a["lru_lambda"]])
    rows = np.concatenate([a["q_norm"].reshape(-1), a["k_norm"].reshape(-1), a["sinks"].reshape(-1),
                           a["router_b"].reshape(-1)])
    arrays = {
        "xT": a["x"][0].T.reshape(KT, P, T).transpose(1, 0, 2),
        "pT": a["p"][:, 0].transpose(0, 2, 1).reshape(DEPTH, PLE // P, P, T).transpose(0, 2, 1, 3),
        "cols": feature_cols(cols),
        "rows": np.broadcast_to(rows[None, :], (P, rows.shape[0])),
        "relT": a["rel_bias"].T,
        "w_rg": a["w_rg"].reshape(DEPTH, KT, 2, HD, HD).transpose(0, 2, 3, 1, 4).reshape(DEPTH, P, KT, HD),
        "w_ig": a["w_ig"].reshape(DEPTH, KT, 2, HD, HD).transpose(0, 2, 3, 1, 4).reshape(DEPTH, P, KT, HD),
        "router": a["router_w"][0].reshape(KT, P, EXPERTS).transpose(1, 0, 2),
        "mix_w": np.stack(mix).reshape(DEPTH, MIX_CHUNKS, P, CHUNK),
        "dense_w": np.stack(ffn_blocks(a["dense_w1"][0], a["dense_w3"][0], a["dense_w2"][0])),
        "moe_w": np.stack(moe).reshape(EXPERTS, FFN_CHUNKS, P, CHUNK),
        "ple_w": np.stack([column_chunks(a["ple_gate_w"][l]) for l in range(DEPTH)]),
        "ple_p": a["ple_proj_w"].reshape(DEPTH, PLE // P, P, D).transpose(0, 2, 1, 3).reshape(DEPTH, P, 2 * D),
    }
    nc = _bacc.Bacc("TRN2", target_bir_lowering=False, num_devices=1)
    arrays = {f"in_{k}": asc(v) for k, v in arrays.items()}
    args = [nc.dram_tensor(k, v.shape, mybir.dt.from_np(v.dtype), kind="ExternalInput").ap() for k, v in arrays.items()]
    bias_line = nc.dram_tensor("bias_line", (HEADS, U_LEN), F32)
    out = nc.dram_tensor("out_T", (P, KT, T), F32, kind="ExternalOutput").ap()
    trunk(nc, *args, bias_line, out)
    r = _run(nc, [arrays], core_ids=[0])
    got = r.results[0]["out_T"]
    return np.ascontiguousarray(got.transpose(2, 1, 0).reshape(1, T, D))
```
